# Optimizing a Trainium2 kernel written in Bass

```python
import math
import jax
import jax.numpy as jnp
from jax import lax
import numpy as np

D_MODEL = 1024
BATCH = 1
SEQ = 2048
DEPTH = 1

N_MIXERS = 2
N_SSM_LAYERS = (DEPTH + N_MIXERS - 1) // N_MIXERS
N_ATTN_LAYERS = DEPTH // N_MIXERS

SSM_WIDTH = D_MODEL
SSM_GROUP = 16
SSM_GROUPS = SSM_WIDTH // SSM_GROUP
SSM_STATE = 64
DT_MIN = 1e-3
DT_MAX = 1e-1

ATT_HEADS = 8
HEAD_DIM = D_MODEL // ATT_HEADS
MOBA_BLOCK = 256
MOBA_TOPK = 3
Q_CHUNK = 32

N_GROUPS = 4
EXPERTS_PER_GROUP = 8
N_EXPERTS = N_GROUPS * EXPERTS_PER_GROUP
EXPERT_TOPK = 2
EXPERT_FF = D_MODEL // 2
ROW_BLOCK = 128

RMS_EPS = 1e-6
NEG_INF = -1e30

kernel_name = 'hybrid_s5_moba_hmoe'

def rmsnorm(x, g):
    xf = x.astype(jnp.float32)
    y = xf * lax.rsqrt(jnp.mean(xf * xf, axis=-1, keepdims=True) + RMS_EPS)
    return (y * g.astype(jnp.float32)).astype(x.dtype)

def _ssm_combine(left, right):
    a1r, a1i, b1r, b1i = left
    a2r, a2i, b2r, b2i = right
    return (a2r * a1r - a2i * a1i,
            a2r * a1i + a2i * a1r,
            a2r * b1r - a2i * b1i + b2r,
            a2r * b1i + a2i * b1r + b2i)

def s5_mixer(h, w_in, lam_re, lam_im, log_dt, b_re, b_im, c_re, c_im, d_skip, w_out):
    f32 = jnp.float32
    bsz, s, _ = h.shape
    u = (h @ w_in).astype(f32)
    ug = u.reshape(bsz, s, SSM_GROUPS, SSM_GROUP)
    lr = jnp.minimum(lam_re.astype(f32), -1e-4)
    li = lam_im.astype(f32)
    dt = jnp.exp(log_dt.astype(f32))[:, None]
    mag = jnp.exp(lr * dt)
    abar_re = mag * jnp.cos(li * dt)
    abar_im = mag * jnp.sin(li * dt)
    den = lr * lr + li * li
    nr = abar_re - 1.0
    gam_re = (nr * lr + abar_im * li) / den
    gam_im = (abar_im * lr - nr * li) / den
    br = b_re.astype(f32)
    bi = b_im.astype(f32)
    bb_re = gam_re[..., None] * br - gam_im[..., None] * bi
    bb_im = gam_re[..., None] * bi + gam_im[..., None] * br
    bu_re = jnp.einsum('bsgc,gpc->bsgp', ug, bb_re)
    bu_im = jnp.einsum('bsgc,gpc->bsgp', ug, bb_im)
    a_re = jnp.broadcast_to(abar_re, (1, s, SSM_GROUPS, SSM_STATE))
    a_im = jnp.broadcast_to(abar_im, (1, s, SSM_GROUPS, SSM_STATE))
    _, _, xr, xi = lax.associative_scan(_ssm_combine, (a_re, a_im, bu_re, bu_im), axis=1)
    y = (jnp.einsum('bsgp,gcp->bsgc', xr, c_re.astype(f32))
         - jnp.einsum('bsgp,gcp->bsgc', xi, c_im.astype(f32)))
    y = y.reshape(bsz, s, SSM_WIDTH) + d_skip.astype(f32) * u
    z = jax.nn.gelu(y).astype(h.dtype)
    vg = z @ w_out
    v, g = jnp.split(vg, 2, axis=-1)
    return v * jax.nn.sigmoid(g)

def moba_mixer(h, w_qkv, w_o):
    f32 = jnp.float32
    bsz, s, _ = h.shape
    qkv = (h @ w_qkv).reshape(bsz, s, 3, ATT_HEADS, HEAD_DIM)
    q = qkv[:, :, 0].transpose(0, 2, 1, 3)
    k = qkv[:, :, 1].transpose(0, 2, 1, 3)
    v = qkv[:, :, 2].transpose(0, 2, 1, 3)
    nb = -(-s // MOBA_BLOCK)
    pad = nb * MOBA_BLOCK - s
    kb = jnp.pad(k, ((0, 0), (0, 0), (0, pad), (0, 0))).reshape(bsz, ATT_HEADS, nb, MOBA_BLOCK, HEAD_DIM)
    vb = jnp.pad(v, ((0, 0), (0, 0), (0, pad), (0, 0))).reshape(bsz, ATT_HEADS, nb, MOBA_BLOCK, HEAD_DIM)
    kmean = jnp.mean(kb.astype(f32), axis=3)
    gate = jnp.einsum('bhsd,bhnd->bhsn', q.astype(f32), kmean)
    cur = jnp.arange(s) // MOBA_BLOCK
    past = jnp.arange(nb)[None, :] < cur[:, None]
    gate = jnp.where(past, gate, NEG_INF)
    k_sel = min(MOBA_TOPK, nb)
    _, idx = lax.top_k(gate, k_sel)
    sel_valid = idx < cur[None, None, :, None]
    scale = HEAD_DIM ** -0.5
    b_ix = jnp.arange(bsz)[:, None, None, None]
    h_ix = jnp.arange(ATT_HEADS)[None, :, None, None]

    def chunk(c):
        q0 = c * Q_CHUNK
        qc = lax.dynamic_slice_in_dim(q, q0, Q_CHUNK, axis=2)
        ic = lax.dynamic_slice_in_dim(idx, q0, Q_CHUNK, axis=2)
        vc = lax.dynamic_slice_in_dim(sel_valid, q0, Q_CHUNK, axis=2)
        k_g = kb[b_ix, h_ix, ic]
        v_g = vb[b_ix, h_ix, ic]
        s_sel = jnp.einsum('bhqd,bhqkld->bhqkl', qc, k_g).astype(f32) * scale
        s_sel = jnp.where(vc[..., None], s_sel, NEG_INF).reshape(bsz, ATT_HEADS, Q_CHUNK, k_sel * MOBA_BLOCK)
        own = q0 // MOBA_BLOCK
        k_own = lax.dynamic_index_in_dim(kb, own, axis=2, keepdims=False)
        v_own = lax.dynamic_index_in_dim(vb, own, axis=2, keepdims=False)
        s_own = jnp.einsum('bhqd,bhld->bhql', qc, k_own).astype(f32) * scale
        qpos = q0 + jnp.arange(Q_CHUNK)
        kpos = own * MOBA_BLOCK + jnp.arange(MOBA_BLOCK)
        s_own = jnp.where(kpos[None, :] <= qpos[:, None], s_own, NEG_INF)
        p = jax.nn.softmax(jnp.concatenate([s_sel, s_own], axis=-1), axis=-1)
        p_sel = p[..., :k_sel * MOBA_BLOCK].reshape(bsz, ATT_HEADS, Q_CHUNK, k_sel, MOBA_BLOCK).astype(v.dtype)
        p_own = p[..., k_sel * MOBA_BLOCK:].astype(v.dtype)
        return (jnp.einsum('bhqkl,bhqkld->bhqd', p_sel, v_g)
                + jnp.einsum('bhql,bhld->bhqd', p_own, v_own))

    o = lax.map(chunk, jnp.arange(s // Q_CHUNK))
    o = o.transpose(1, 0, 3, 2, 4).reshape(bsz, s, ATT_HEADS * HEAD_DIM)
    return o @ w_o

def hier_moe(h, w_group, w_expert, w1, w3, w2):
    f32 = jnp.float32
    bsz, s, d = h.shape
    n = bsz * s
    xt = h.reshape(n, d)
    g_prob = jax.nn.softmax((xt @ w_group).astype(f32), axis=-1)
    g_gate, g_idx = lax.top_k(g_prob, 1)
    e_logits = (xt @ w_expert).astype(f32).reshape(n, N_GROUPS, EXPERTS_PER_GROUP)
    e_in = e_logits[jnp.arange(n), g_idx[:, 0]]
    e_gate, e_local = lax.top_k(jax.nn.softmax(e_in, axis=-1), EXPERT_TOPK)
    e_gate = e_gate / jnp.sum(e_gate, axis=-1, keepdims=True)
    gates = (g_gate * e_gate).reshape(-1)
    expert_id = (g_idx * EXPERTS_PER_GROUP + e_local).reshape(-1).astype(jnp.int32)
    nk = n * EXPERT_TOPK
    order = jnp.argsort(expert_id)
    sorted_e = expert_id[order]
    counts = jnp.bincount(expert_id, length=N_EXPERTS)
    starts = jnp.cumsum(counts) - counts
    padded = ((counts + ROW_BLOCK - 1) // ROW_BLOCK) * ROW_BLOCK
    pad_end = jnp.cumsum(padded)
    pad_start = pad_end - padded
    dest = pad_start[sorted_e] + (jnp.arange(nk) - starts[sorted_e])
    cap = nk + N_EXPERTS * ROW_BLOCK
    n_blk = cap // ROW_BLOCK
    row_token = jnp.zeros((cap,), jnp.int32).at[dest].set((order // EXPERT_TOPK).astype(jnp.int32))
    row_gate = jnp.zeros((cap,), f32).at[dest].set(gates[order])
    blk_start = jnp.arange(n_blk) * ROW_BLOCK
    blk_e = jnp.minimum(jnp.sum(pad_end[None, :] <= blk_start[:, None], axis=1), N_EXPERTS - 1).astype(jnp.int32)
    xr = xt[row_token].reshape(n_blk, ROW_BLOCK, d)

    def expert_block(args):
        xb, e = args
        return (jax.nn.silu(xb @ w1[e]) * (xb @ w3[e])) @ w2[e]

    yr = lax.map(expert_block, (xr, blk_e)).reshape(cap, d)
    out = jnp.zeros((n, d), f32).at[row_token].add(yr.astype(f32) * row_gate[:, None])
    return out.astype(h.dtype).reshape(bsz, s, d)

def setup_inputs(seed: int = 0) -> dict:
    key = jax.random.key(seed)
    ks = jax.random.split(key, 24)
    f32 = jnp.float32

    def nrm(k, shape, scale):
        return jax.random.normal(k, shape, f32) * scale

    G, P, C = SSM_GROUPS, SSM_STATE, SSM_GROUP
    return {
        'x': nrm(ks[0], (BATCH, SEQ, D_MODEL), 1.0),
        'ln_mix': 1.0 + nrm(ks[1], (DEPTH, D_MODEL), 0.02),
        'ln_ffn': 1.0 + nrm(ks[2], (DEPTH, D_MODEL), 0.02),
        'ln_final': 1.0 + nrm(ks[3], (D_MODEL,), 0.02),
        'ssm_w_in': nrm(ks[4], (N_SSM_LAYERS, D_MODEL, SSM_WIDTH), D_MODEL ** -0.5),
        'ssm_lam_re': -0.5 + nrm(ks[5], (N_SSM_LAYERS, G, P), 0.01),
        'ssm_lam_im': math.pi * jnp.arange(P, dtype=f32) + nrm(ks[6], (N_SSM_LAYERS, G, P), 0.01),
        'ssm_log_dt': jax.random.uniform(ks[7], (N_SSM_LAYERS, G), f32, math.log(DT_MIN), math.log(DT_MAX)),
        'ssm_b_re': nrm(ks[8], (N_SSM_LAYERS, G, P, C), (2 * C) ** -0.5),
        'ssm_b_im': nrm(ks[9], (N_SSM_LAYERS, G, P, C), (2 * C) ** -0.5),
        'ssm_c_re': nrm(ks[10], (N_SSM_LAYERS, G, C, P), P ** -0.5),
        'ssm_c_im': nrm(ks[11], (N_SSM_LAYERS, G, C, P), P ** -0.5),
        'ssm_d': nrm(ks[12], (N_SSM_LAYERS, SSM_WIDTH), 0.5),
        'ssm_w_out': nrm(ks[13], (N_SSM_LAYERS, SSM_WIDTH, 2 * D_MODEL), SSM_WIDTH ** -0.5),
        'attn_w_qkv': nrm(ks[14], (N_ATTN_LAYERS, D_MODEL, 3 * ATT_HEADS * HEAD_DIM), D_MODEL ** -0.5),
        'attn_w_o': nrm(ks[15], (N_ATTN_LAYERS, ATT_HEADS * HEAD_DIM, D_MODEL), D_MODEL ** -0.5),
        'moe_w_group': nrm(ks[16], (DEPTH, D_MODEL, N_GROUPS), D_MODEL ** -0.5),
        'moe_w_expert': nrm(ks[17], (DEPTH, D_MODEL, N_EXPERTS), D_MODEL ** -0.5),
        'moe_w1': nrm(ks[18], (DEPTH, N_EXPERTS, D_MODEL, EXPERT_FF), D_MODEL ** -0.5),
        'moe_w3': nrm(ks[19], (DEPTH, N_EXPERTS, D_MODEL, EXPERT_FF), D_MODEL ** -0.5),
        'moe_w2': nrm(ks[20], (DEPTH, N_EXPERTS, EXPERT_FF, D_MODEL), EXPERT_FF ** -0.5),
    }

def reference(x, ln_mix, ln_ffn, ln_final, ssm_w_in, ssm_lam_re, ssm_lam_im, ssm_log_dt,
              ssm_b_re, ssm_b_im, ssm_c_re, ssm_c_im, ssm_d, ssm_w_out, attn_w_qkv, attn_w_o,
              moe_w_group, moe_w_expert, moe_w1, moe_w3, moe_w2):
    h = x
    for i in range(DEPTH):
        hn = rmsnorm(h, ln_mix[i])
        j = i // N_MIXERS
        if i % N_MIXERS == 0:
            mix = s5_mixer(hn, ssm_w_in[j], ssm_lam_re[j], ssm_lam_im[j], ssm_log_dt[j],
                           ssm_b_re[j], ssm_b_im[j], ssm_c_re[j], ssm_c_im[j], ssm_d[j], ssm_w_out[j])
        else:
            mix = moba_mixer(hn, attn_w_qkv[j], attn_w_o[j])
        h = h + mix
        h = h + hier_moe(rmsnorm(h, ln_ffn[i]), moe_w_group[i], moe_w_expert[i],
                         moe_w1[i], moe_w3[i], moe_w2[i])
    return rmsnorm(h, ln_final)


_drawn_inputs = setup_inputs


def setup_inputs(seed=0):
    import zlib

    import numpy as np

    out = dict(_drawn_inputs(seed))
    spreads = {}
    factors = {'ln_mix': 4.073, 'ln_final': 2.997, 'ssm_lam_re': 8.0}
    for name, (base, spread) in spreads.items():
        noise = np.random.default_rng([zlib.crc32(name.encode()), seed]).standard_normal(out[name].shape)
        drawn = base * np.exp(spread * noise) if base else spread * noise
        out[name] = jnp.asarray(drawn.astype(out[name].dtype))
    for name, factor in factors.items():
        out[name] = (out[name] * factor).astype(out[name].dtype)
    return out
```

```python
from contextlib import ExitStack

import concourse.bass as bass
from concourse import mybir

F32 = mybir.dt.float32
F32R = mybir.dt.float32r
I32 = mybir.dt.int32
BF16 = mybir.dt.bfloat16
ALU = mybir.AluOpType
ACT = mybir.ActivationFunctionType
AX = mybir.AxisListType

P = 128
D = 1024
S = 2048
G = 64
C = 16
N = 64
TAU = 8
PR = G // 2
DC = D // P
NT = S // P
GR = 4
EG = 8
NE = GR * EG
FF = D // 2
FC = FF // P
SLOTS = 2 * S + NE * P
NB = SLOTS // P
NBT = NB + 2
EPS = 1e-6
BIG = 1.0e30

BK = 512


def tile_rows(ap, K, tau):
    return ap.rearrange("(k p t) d -> k t p d", k=2, t=TAU)[K, tau]


def same_rows(q):
    g = 8 * (q // 2) + q % 2
    return slice(g, g + 7, 2)


def build_mixer(nc, x, ln_mix, ln_ffn, w_in, lam_re, lam_im, log_dt, b_re, b_im, c_re, c_im,
                d_skip, w_out, w_group, w_expert, h_d, hn_d, W_d, T_d, G_d, ident, rows, gates, blk):
    ctx = ExitStack()
    with ctx:
        def sb(name, shape, dt=F32):
            return ctx.enter_context(nc.sbuf_tensor(name, shape, dt))

        def sem(name):
            return ctx.enter_context(nc.semaphore(name))

        R1 = sb("R1", [P, 8192])
        R2 = sb("R2", [P, 8192])
        R3 = sb("R3", [P, 8192])
        R4 = sb("R4", [P, 8192])
        R5 = sb("R5", [P, 9216])
        R6 = sb("R6", [P, 4096])
        R7 = sb("R7", [P, 6144])
        A4 = sb("A4", [P, 2, 2, PR])
        M4 = sb("M4", [P, 2, 2, PR])
        stats = sb("stats", [P, 64])
        mhalf = sb("mhalf", [P, 2])
        junk = R6[:, 2048:3072]

        w_in_sb = R1[:, :].rearrange("p (k n) -> p k n", k=DC)
        U = [R3[:, :], R4[:, :]]
        St = R5[:, 0:8256].rearrange("p (r q k) -> p r q k", r=2, q=PR)
        LG = R5[:, 8256:8832].rearrange("p (i e) -> p i e", i=NT)
        wr = R5[:, 8832:9120].rearrange("p (k e) -> p k e", k=DC)
        T2 = R5[:, 9120:9184].rearrange("p (r q) -> p r q", r=2)
        xt = [R7[:, 1024 * j:1024 * (j + 1)] for j in range(2)]
        xn = [R7[:, 2048 + 1024 * j:3072 + 1024 * j] for j in range(2)]
        hT = [R7[:, 4096 + 1024 * j:5120 + 1024 * j] for j in range(2)]
        wb = [R6[:, 1024 * j:1024 * (j + 1)] for j in range(2)]
        tgb = [R6[:, 2048 * j:2048 * (j + 1)] for j in range(2)]
        sg = R6[:, 0:1024]
        hn2 = R6[:, 1024:2048]
        hn2T = R6[:, 2048:3072]
        gB = R6[:, 3072:4096]
        ssq = stats[:, 0:16]
        rstd = stats[:, 16:32]
        ssq2 = stats[:, 32:48]
        rstd2 = stats[:, 48:64]

        TP = ctx.enter_context(nc.psum_tensor("TP", [P, D], F32))
        UP = [ctx.enter_context(nc.psum_tensor(f"UP{j}", [P, D], F32)) for j in range(2)]
        AX2 = [ctx.enter_context(nc.psum_tensor(f"AX{j}", [P, BK], F32)) for j in range(2)]

        E = R3[:, 0:576].rearrange("p (r q j) -> p r q j", r=2, q=PR)
        Er = R3[:, 576:1088].rearrange("p (r q j) -> p r q j", r=2, q=PR)
        cf = R3[:, 1088:1216].rearrange("p (v q) -> p v q", v=4)
        Bb = R3[:, 1216:2240].rearrange("p (r q c) -> p r q c", r=2, q=PR)
        Cs = R3[:, 2240:3264].rearrange("p (r q c) -> p r q c", r=2, q=PR)
        Braw = R3[:, 3264:4288].rearrange("p (r q c) -> p r q c", r=2, q=PR)
        tw = R3[:, 4288:5440]
        tz = R3[:, 5440:6592]
        Dc = R3[0:C, 6592:6656]
        dstep = R3[0:C, 6656:7680].rearrange("p (g c) -> p g c", g=G)
        zero = R3[:, 6656:7680]
        L = R2[0:PR, 0:128]
        pv = R2[0:PR, 0:4096].rearrange("p (v n) -> p v n", v=32)
        Cn = R2[:, 4096:5120].rearrange("p (r t n) -> p r t n", r=2, t=4)
        Wst = R4[:, :].rearrange("p (r q t c) -> p r q t c", r=2, q=PR, t=TAU)
        KR = R4[0:C, :].rearrange("p (g m) -> p g m", g=G)
        Gst = R5[:, :].rearrange("p (r q j c) -> p r q j c", r=2, q=PR, j=TAU + 1)

        at = [0]

        def rv(*shape):
            n = 1
            for d in shape:
                n *= d
            v = R2[:, at[0]:at[0] + n]
            at[0] += n
            names = "abcd"[:len(shape)]
            return v.rearrange("p (" + " ".join(names) + ") -> p " + " ".join(names),
                               **{c: d for c, d in zip(names, shape)}) if len(shape) > 1 else v

        rt_og, rt_d = rv(NT, GR), rv(NT, GR)
        rt_o1, rt_o2, rt_c, rt_ein = rv(NT, EG), rv(NT, EG), rv(NT, EG), rv(NT, EG)
        rt_gm, rt_mn, rt_m1, rt_m2, rt_x = rv(NT), rv(NT), rv(NT), rv(NT), rv(NT)
        rt_e4 = rv(NT, EG, GR)
        rt_M1, rt_M2, rt_M, rt_P, rt_S = rv(NT, NE), rv(NT, NE), rv(NT, NE), rv(NT, NE), rv(NT, NE)
        rt_tot, rt_nb, rt_one, rt_be, rt_bs = rv(NE), rv(NE), rv(NE), rv(NE), rv(NE)
        rt_ci = rv(NE).bitcast(I32)
        rt_sf = rv(NT, 2)
        slots = rv(NT, 2).bitcast(I32)
        rt_lo, rt_hi = rv(NT, 2).bitcast(I32), rv(NT, 2).bitcast(I32)
        rt_bk = rv(NBT, NE)
        rt_eb = rv(3, NBT)
        assert at[0] <= 8192 and NBT < P
        tri, ones = R4[:, 0:P], R4[:, P:2 * P]
        ioi = R4[:, 256:256 + P].bitcast(I32)
        iof = R4[:, 384:384 + P]
        tid = R4[:, 512:512 + 2 * NT].bitcast(I32)
        zi = R4[:, 600:600 + NBT].bitcast(I32)
        tidf = R4[:, 700:700 + 2 * NT].rearrange("p (i j) -> p i j", j=2)
        zf = R4[:, 800:800 + NBT]
        lof = R4[:, 900:900 + 2 * NT].rearrange("p (i j) -> p i j", j=2)
        hif = R4[:, 950:950 + 2 * NT].rearrange("p (i j) -> p i j", j=2)
        free = R4[:, 1000:1000 + NBT]
        ohP = R1[:, 0:2 * NT * P].rearrange("p (i j m) -> p i j m", i=NT, j=2)
        ohB = R1[:, 2 * NT * P:2 * NT * (P + NBT)].rearrange("p (i j b) -> p i j b", i=NT, j=2)

        s_par = sem("params_loaded")
        s_bc = sem("b_and_d_loaded")
        s_c = sem("c_loaded")
        s_win = sem("w_in_loaded")
        s_gm = sem("gain_loaded")
        s_wing = sem("w_in_scaled")
        s_ident = sem("ident_ready")
        s_zero = sem("zero_ready")
        s_x = [sem(f"x_loaded{j}") for j in range(2)]
        s_sq = sem("squares_summed")
        s_rs = sem("rstd_ready")
        s_xn = sem("xn_ready")
        s_tp = sem("x_transposed")
        s_hT = sem("hT_ready")
        s_mm = sem("u_product")
        s_ue = sem("u_stored")
        s_act = sem("setup_act")
        s_dve = sem("dve_chain")
        s_pow = sem("powers_ready")
        s_pt = sem("params_transposed")
        s_ct = sem("c_transposed")
        s_cc = sem("c_copied")
        s_Wr = sem("W_products")
        s_Gr = sem("G_products")
        s_wt = sem("W_transposed")
        s_wc = sem("W_copied")
        s_wd = [sem(f"W_stored{j}") for j in range(2)]
        s_tz = sem("T_zeroed")
        s_kr = sem("KR_product")
        s_kc = sem("KR_copied")
        s_krd = sem("KR_with_skip")
        s_td = sem("T_stored")
        s_gd = sem("G_stored")
        s_ut = sem("u_transposed")
        s_uv = sem("U_copied_dve")
        s_ua = sem("U_copied_act")
        s_wl = [sem(f"W_loaded{j}") for j in range(2)]
        s_v = sem("states_collected")
        s_vr = sem("states_re_copied")
        s_vi = sem("states_im_copied")
        s_s0 = sem("carry_ready")
        s_sc = sem("scan_steps")
        s_scd = sem("scan_done")
        s_tg = [sem(f"TG_loaded{j}") for j in range(2)]
        s_y = sem("y_product")
        s_z = sem("z_ready")
        s_wo = sem("w_out_loaded")
        s_zt = sem("z_transposed")
        s_zc = sem("zT_ready")
        s_vg = sem("vg_product")
        s_th = sem("tanh_ready")
        s_hh = sem("h_ready")
        s_g1 = sem("gate_half")
        s_x2 = [sem(f"x2_loaded{j}") for j in range(2)]
        s_sq2 = sem("h_squares")
        s_rs2 = sem("h_rstd")
        s_hn = sem("hn_ready")
        s_hd = [sem(f"h_stored{j}") for j in range(2)]
        s_hnd = sem("hn_stored")
        s_ht = sem("hn_transposed")
        s_hc = sem("hnT_ready")
        s_lg = sem("logits_product")
        s_lc = sem("logits_copied")
        s_gf = sem("ffn_gain_loaded")
        s_wrl = sem("router_weights_loaded")
        s_rt = sem("routing_steps")
        s_re = sem("routing_exponentials")
        s_rk = sem("ranks_ready")
        s_tri = sem("routing_constants")
        s_tb = sem("slots_table")

        xdma = lambda i: tile_rows(x, i // TAU, i % TAU)
        W_v = W_d.rearrange("(b p) n -> b p n", p=P)
        T_v = T_d.rearrange("p (b n) -> b p n", b=8)
        G_v = G_d.rearrange("(r p) (b n) -> b r p n", r=2, b=8)

        block = ctx.enter_context(nc.Block())

        @block.sync
        def _(sp):
            sp.dma_start(pv[:, 0, :], lam_re.rearrange("(q a) n -> q (a n)", a=2)).then_inc(s_par, 16)
            sp.dma_start(pv[:, 1, :], lam_im.rearrange("(q a) n -> q (a n)", a=2)).then_inc(s_par, 16)
            sp.dma_start(pv[:, 2, 0:2], log_dt.rearrange("(q a) -> q a", a=2)).then_inc(s_par, 16)
            sp.dma_start(xt[0], xdma(0)).then_inc(s_x[0], 16)
            sp.dma_start(w_in_sb, w_in.rearrange("(k p) n -> p k n", p=P)).then_inc(s_win, 16)
            sp.dma_start(xt[1], xdma(1)).then_inc(s_x[1], 16)
            sp.wait_ge(s_zero, 1)
            for b in range(8):
                sp.dma_start(T_v[b], zero).then_inc(s_tz, 16)

            def load_x(i):
                sp.wait_ge(s_xn, i - 1)
                sp.dma_start(xt[i % 2], xdma(i)).then_inc(s_x[i % 2], 16)

            for i in range(2, TAU + 2):
                load_x(i)
            for b in range(8):
                sp.wait_ge(s_wc, 4 * b + 4)
                sp.dma_start(W_v[b], wb[b % 2]).then_inc(s_wd[b % 2], 16)
            sp.wait_ge(s_Gr, 2)
            for r in range(2):
                sp.dma_start(G_d.rearrange("(r p) (q x) -> r p q x", r=2, x=P)[r],
                             Gst[:, r, :, 1:9, :].rearrange("p q j c -> p q (j c)")).then_inc(s_gd, 16)
            sp.wait_ge(s_krd, 1)
            sp.wait_ge(s_tz, 16 * 8)
            for t in range(TAU):
                sp.dma_start(T_d.rearrange("(t c) (g m) -> t c g m", t=TAU, g=G)[t][:, :, C * t:P],
                             KR[:, :, 0:P - C * t]).then_inc(s_td, 16)

            def load_w(K):
                for b in range(8):
                    if b >= 2 or K == 1:
                        sp.wait_ge(s_v, 16 * K + 2 * (b - 2) + 2)
                    elif K == 0:
                        sp.wait_ge(s_wd[0], 64)
                        sp.wait_ge(s_wd[1], 64)
                    sp.dma_start(wb[b % 2], W_v[b]).then_inc(s_wl[b % 2], 16)

            def load_tg(K):
                for b in range(8):
                    if b >= 2:
                        sp.wait_ge(s_y, 16 * K + 2 * (b - 2) + 2)
                    t = tgb[b % 2]
                    sp.dma_start(t[:, 0:1024], T_v[b]).then_inc(s_tg[b % 2], 16)
                    sp.dma_start(t[:, 1024:1536], G_v[b, 0]).then_inc(s_tg[b % 2], 16)
                    sp.dma_start(t[:, 1536:2048], G_v[b, 1]).then_inc(s_tg[b % 2], 16)

            load_w(0)
            for i in range(TAU + 2, NT):
                load_x(i)
            sp.wait_ge(s_mm, NT)
            wo_v = w_out.rearrange("(k p) n -> p k n", p=P)
            sp.dma_start(R1[:, :].rearrange("p (k n) -> p k n", k=4), wo_v[:, 0:4, :]).then_inc(s_wo, 16)
            sp.wait_ge(s_gd, 32)
            sp.wait_ge(s_td, 16 * 8)
            sp.wait_ge(s_v, 16)
            load_tg(0)
            sp.wait_ge(s_y, 16)
            load_w(1)
            sp.dma_start(R3[:, :].rearrange("p (k n) -> p k n", k=4), wo_v[:, 4:8, :]).then_inc(s_wo, 16)

            def load_x2(i):
                if i >= 2:
                    sp.wait_ge(s_hh, 2 * (i - 2) + 2)
                else:
                    sp.wait_ge(s_xn, NT)
                sp.dma_start(xt[i % 2], xdma(i)).then_inc(s_x2[i % 2], 16)

            def gate_tiles(K):
                for i in range(TAU * K, TAU * K + TAU):
                    if K == 0 and i == 0:
                        load_x2(0)
                        load_x2(1)
                        sp.wait_ge(s_v, 32)
                    if i == TAU * K:
                        sp.dma_start(gB, ln_ffn.partition_broadcast(P)).then_inc(s_gf, 16)
                    sp.wait_ge(s_hh, 2 * i + 2)
                    sp.dma_start(tile_rows(h_d, i // TAU, i % TAU), xn[i % 2]).then_inc(s_hd[i % 2], 16)
                    if i + 2 < NT:
                        load_x2(i + 2)
                    sp.wait_ge(s_hn, i + 1)
                    sp.dma_start(tile_rows(hn_d, i // TAU, i % TAU), hn2).then_inc(s_hnd, 16)

            gate_tiles(0)
            sp.wait_ge(s_hnd, 16 * TAU)
            sp.wait_ge(s_hc, TAU)
            sp.wait_ge(s_lg, TAU)
            load_tg(1)
            sp.wait_ge(s_y, 32)
            gate_tiles(1)
            sp.wait_ge(s_hnd, 16 * NT)
            for j in range(2):
                sp.wait_ge(s_hd[j], 16 * NT // 2)

        @block.gpsimd
        def _(pool):
            nc.gpsimd.memset(ident[:, :], 0.0).then_inc(s_ident, 1)
            nc.gpsimd.memset(mhalf[:, :], -0.5).then_inc(s_ident, 1)
            nc.gpsimd.memset(zero, 0.0).then_inc(s_zero, 1)
            pool.wait_ge(s_ident, 2)
            nc.gpsimd.affine_select(out=ident[:, :], in_=ident[:, :], compare_op=ALU.not_equal, fill=1.0,
                                    base=0, pattern=[[-1, P]], channel_multiplier=1).then_inc(s_ident, 1)
            pool.wait_ge(s_ident, 3)
            with nc.allow_non_contiguous_dma(reason="a few thousand parameters"):
                gmixT = M4[:, 0, 0, 0:DC]
                pool.dma_start(gmixT, ln_mix.rearrange("(k p) -> p k", p=P)).then_inc(s_gm, 16)
                for a in range(2):
                    for r, src in enumerate((b_re, b_im)):
                        pool.dma_start(Braw[N * a:N * a + N, r], src.rearrange("(q a) n c -> a n q c", a=2)[a]).then_inc(s_bc, 16)
                pool.dma_start(Dc, d_skip.rearrange("(g c) -> c g", c=C)).then_inc(s_bc, 16)

            def stat(i, src, dst, s_from, s_to):
                pool.wait_ge(s_from, i + 1)
                nc.gpsimd.tensor_scalar(dst[:, i:i + 1], src[:, i:i + 1], 1.0 / D, EPS, ALU.mult, ALU.add).then_inc(s_to, 1)
                pool.wait_ge(s_to, 2 * i + 1)
                nc.gpsimd.tensor_tensor(out=dst[:, i:i + 1], in0=dst[:, i:i + 1], in1=mhalf[:, 0:1], op=ALU.pow).then_inc(s_to, 1)

            for i in range(NT):
                stat(i, ssq, rstd, s_sq, s_rs)
            with nc.allow_non_contiguous_dma(reason="router weights"):
                pool.wait_ge(s_gd, 32)
                pool.dma_start(wr[:, :, 0:GR], w_group.rearrange("(k p) e -> p k e", p=P)).then_inc(s_wrl, 16)
                pool.dma_start(wr[:, :, GR:GR + NE], w_expert.rearrange("(k p) e -> p k e", p=P)).then_inc(s_wrl, 16)
            for i in range(NT):
                if i == TAU:
                    pool.wait_ge(s_y, 32)
                    nc.gpsimd.memset(ones, 1.0).then_inc(s_tri, 1)
                    pool.wait_ge(s_tri, 1)
                    nc.gpsimd.affine_select(out=tri, in_=ones, compare_op=ALU.is_gt, fill=0.0, base=0,
                                            pattern=[[1, P]], channel_multiplier=-1).then_inc(s_tri, 1)
                    nc.gpsimd.iota(ioi, pattern=[[1, P]], base=0, channel_multiplier=0).then_inc(s_tri, 1)
                    nc.gpsimd.iota(tid, pattern=[[S // 2, 2], [1, TAU], [S, 2]], base=1, channel_multiplier=TAU).then_inc(s_tri, 1)
                    nc.gpsimd.iota(zi, pattern=[[P, NBT]], base=2 * S + 1, channel_multiplier=1).then_inc(s_tri, 1)
                stat(i, ssq2, rstd2, s_sq2, s_rs2)

        @block.scalar
        def _(act):
            for r, src in enumerate((c_re, c_im)):
                v = src.rearrange("(t q a) c n -> t a q c n", t=4, a=2)
                for t in range(4):
                    for a in range(2):
                        act.dma_start(Cn[:, r, t, N * a:N * a + N], v[t, a]).then_inc(s_c, 16)
            act.wait_ge(s_par, 48)
            nc.scalar.activation(pv[:, 3, 0:2], pv[:, 2, 0:2], ACT.Exp).then_inc(s_act, 1)
            act.wait_ge(s_dve, 3)
            nc.scalar.activation(pv[:, 7, :], pv[:, 5, :], ACT.Exp).then_inc(s_act, 1)
            act.wait_ge(s_dve, 13)
            nc.scalar.activation(pv[:, 12, :], pv[:, 9, :], ACT.Sin).then_inc(s_act, 1)
            nc.scalar.activation(pv[:, 13, :], pv[:, 10, :], ACT.Sin).then_inc(s_act, 1)

            def square(i):
                act.wait_ge(s_x[i % 2], 16 * (i // 2 + 1))
                if i > 0:
                    act.wait_ge(s_sq, i)
                nc.scalar.activation(junk, xt[i % 2], ACT.Square, accum_out=ssq[:, i:i + 1]).then_inc(s_sq, 1)

            def normalise(i):
                act.wait_ge(s_rs, 2 * i + 2)
                if i >= 2:
                    act.wait_ge(s_tp, i - 1)
                nc.scalar.activation(xn[i % 2], xt[i % 2], ACT.Copy, scale=rstd[:, i:i + 1]).then_inc(s_xn, 1)

            def copy_hT(i):
                act.wait_ge(s_tp, i + 1)
                if i >= 2:
                    act.wait_ge(s_mm, i - 1)
                nc.scalar.activation(hT[i % 2], TP[:, :], ACT.Copy).then_inc(s_hT, 1)

            def store_u(i):
                act.wait_ge(s_mm, i + 1)
                if i == TAU:
                    act.wait_ge(s_ut, 16)
                if i == 0:
                    act.wait_ge(s_ct, 2)
                    act.wait_ge(s_pt, 1)
                nc.scalar.activation(R2[:, :].rearrange("p (g t c) -> p t g c", g=G, t=TAU)[:, i % TAU],
                                     UP[i % 2][:, :].rearrange("p (g c) -> p g c", g=G), ACT.Copy).then_inc(s_ue, 1)

            def copy_U(K):
                for q in range(1, 16, 2):
                    act.wait_ge(s_ut, 16 * K + q + 1)
                    nc.scalar.activation(U[K][:, BK * q:BK * q + BK], AX2[q % 2][:, :], ACT.Copy).then_inc(s_ua, 1)

            def copy_states_im(K):
                for q in range(16):
                    act.wait_ge(s_v, 16 * K + q + 1)
                    if q == 0:
                        act.wait_ge(s_s0, K + 1)
                    ps = AX2[q % 2][N:P, :].rearrange("n (q a k) -> n q a k", q=2, a=2)
                    for a in range(2):
                        last = nc.scalar.activation(St[N * a:N * a + N, 1, 2 * q:2 * q + 2, 1:129], ps[:, :, a, :], ACT.Copy)
                    last.then_inc(s_vi, 1)

            def phase1(K):
                for i in range(TAU * K, TAU * K + TAU):
                    if i + 1 < NT:
                        copy_hT(i + 1)
                    if i + 2 < NT:
                        square(i + 2)
                        normalise(i + 2)
                    store_u(i)

            square(0)
            normalise(0)
            copy_hT(0)
            square(1)
            normalise(1)
            phase1(0)
            for q in range(16):
                act.wait_ge(s_wt, q + 1)
                b = q // 2
                if b >= 2 and q % 2 == 0:
                    act.wait_ge(s_wd[b % 2], 16 * (b // 2))
                for l in range(2):
                    dst = wb[b % 2].rearrange("p (q a r n) -> p q r a n", q=4, a=2, r=2)[:, 2 * (q % 2) + l]
                    nc.scalar.activation(dst, AX2[q % 2][:, 256 * l:256 * l + 256].rearrange("p (r a n) -> p r a n", r=2, a=2),
                                         ACT.Copy).then_inc(s_wc, 1)
            copy_U(0)
            copy_states_im(0)
            phase1(1)
            copy_U(1)

            def gelu(K):
                for q in range(16):
                    act.wait_ge(s_y, 16 * K + q + 1)
                    z = R2[:, :].rearrange("p (t g c) -> p g t c", t=TAU, g=G)[:, same_rows(q)]
                    if q == 0:
                        act.wait_ge(s_ut, 32)
                        if K == 1:
                            act.wait_ge(s_zt, TAU)
                    nc.scalar.activation(z, AX2[q % 2][:, :].rearrange("p (g t c) -> p g t c", g=4, t=TAU),
                                         ACT.Gelu_apprx_tanh).then_inc(s_z, 1)

            def tanh_half(i, nh):
                act.wait_ge(s_vg, 2 * i + nh + 1)
                if i >= 1:
                    act.wait_ge(s_hh, 2 * (i - 1) + nh + 1)
                nc.scalar.activation(sg[:, BK * nh:BK * nh + BK], UP[nh][:, BK:2 * BK], ACT.Tanh, scale=0.5).then_inc(s_th, 1)

            def square_h(i):
                act.wait_ge(s_hh, 2 * i + 2)
                nc.scalar.activation(R2[:, D * (i % TAU):D * (i % TAU) + D], xn[i % 2], ACT.Square,
                                     accum_out=ssq2[:, i:i + 1]).then_inc(s_sq2, 1)

            def copy_zT(i):
                act.wait_ge(s_zt, i + 1)
                nc.scalar.activation(hT[i % 2], TP[:, :], ACT.Copy).then_inc(s_zc, 1)

            def copy_hnT(i):
                act.wait_ge(s_ht, i + 1)
                if i >= 1:
                    act.wait_ge(s_lg, i)
                nc.scalar.activation(hn2T, TP[:, :], ACT.Copy).then_inc(s_hc, 1)

            def copy_logits(i):
                act.wait_ge(s_lg, i + 1)
                nc.scalar.activation(LG[:, i, :], AX2[0][:, 0:GR + NE], ACT.Copy).then_inc(s_lc, 1)

            for K in range(2):
                gelu(K)
                if K == 0:
                    copy_states_im(1)
                t0 = TAU * K
                copy_zT(t0)
                for i in range(t0, t0 + TAU):
                    if i > t0:
                        copy_hnT(i - 1)
                    tanh_half(i, 0)
                    if i > t0:
                        copy_logits(i - 1)
                    if i + 1 < t0 + TAU:
                        copy_zT(i + 1)
                    tanh_half(i, 1)
                    square_h(i)
                copy_hnT(t0 + TAU - 1)
                copy_logits(t0 + TAU - 1)
            act.wait_ge(s_rt, 1)
            nc.scalar.activation(rt_d, rt_d, ACT.Exp).then_inc(s_re, 1)
            act.wait_ge(s_rt, 2)
            nc.scalar.activation(rt_x, rt_x, ACT.Exp).then_inc(s_re, 1)

        @block.vector
        def _(dve):
            chain = [0]

            def link(ins):
                chain[0] += 1
                ins.then_inc(s_dve, 1)
                dve.wait_ge(s_dve, chain[0])

            def dt_of(ap):
                return ap[:, :].unsqueeze(2).broadcast_to([PR, 2, N])

            v2 = lambda j: pv[:, j, :].rearrange("q (a n) -> q a n", a=2)
            ts, tt = nc.vector.tensor_scalar, nc.vector.tensor_tensor
            dve.wait_ge(s_par, 48)
            link(ts(pv[:, 4, :], pv[:, 0, :], -1e-4, None, ALU.min))
            dve.wait_ge(s_act, 1)
            link(tt(out=v2(5), in0=v2(4), in1=dt_of(pv[:, 3, 0:2]), op=ALU.mult))
            link(tt(out=v2(6), in0=v2(1), in1=dt_of(pv[:, 3, 0:2]), op=ALU.mult))
            MAGIC = 12582912.0
            link(ts(pv[:, 8, :], pv[:, 6, :], 0.15915494309189535, MAGIC, ALU.mult, ALU.add))
            link(ts(pv[:, 8, :], pv[:, 8, :], -MAGIC, None, ALU.add))
            link(ts(pv[:, 9, :], pv[:, 8, :], -6.28125, None, ALU.mult))
            link(tt(out=pv[:, 9, :], in0=pv[:, 9, :], in1=pv[:, 6, :], op=ALU.add))
            for part in (0.0019350051879882812, 3.019916050561733e-07):
                link(nc.vector.scalar_tensor_tensor(out=pv[:, 9, :], in0=pv[:, 8, :], scalar=-part, in1=pv[:, 9, :],
                                                    op0=ALU.mult, op1=ALU.add))
            link(ts(pv[:, 9, :], pv[:, 9, :], 3.1415925, -3.1415925, ALU.min, ALU.max))
            link(ts(pv[:, 10, :], pv[:, 9, :], -1.0, None, ALU.mult))
            link(tt(out=pv[:, 10, :], in0=pv[:, 10, :], in1=pv[:, 9, :], op=ALU.max))
            link(ts(pv[:, 10, :], pv[:, 10, :], -1.0, 1.5707963267948966, ALU.mult, ALU.add))
            assert chain[0] == 13
            link(tt(out=pv[:, 14, :], in0=pv[:, 4, :], in1=pv[:, 4, :], op=ALU.mult))
            link(tt(out=pv[:, 15, :], in0=pv[:, 1, :], in1=pv[:, 1, :], op=ALU.mult))
            link(tt(out=pv[:, 14, :], in0=pv[:, 14, :], in1=pv[:, 15, :], op=ALU.add))
            link(nc.vector.reciprocal(pv[:, 14, :], pv[:, 14, :]))
            dve.wait_ge(s_act, 4)
            link(tt(out=pv[:, 16, :], in0=pv[:, 7, :], in1=pv[:, 13, :], op=ALU.mult))
            link(tt(out=pv[:, 17, :], in0=pv[:, 7, :], in1=pv[:, 12, :], op=ALU.mult))
            link(ts(pv[:, 20, :], pv[:, 16, :], -1.0, None, ALU.add))
            link(tt(out=pv[:, 21, :], in0=pv[:, 20, :], in1=pv[:, 4, :], op=ALU.mult))
            link(tt(out=pv[:, 22, :], in0=pv[:, 17, :], in1=pv[:, 1, :], op=ALU.mult))
            link(tt(out=pv[:, 21, :], in0=pv[:, 21, :], in1=pv[:, 22, :], op=ALU.add))
            link(tt(out=pv[:, 18, :], in0=pv[:, 21, :], in1=pv[:, 14, :], op=ALU.mult))
            link(tt(out=pv[:, 21, :], in0=pv[:, 17, :], in1=pv[:, 4, :], op=ALU.mult))
            link(tt(out=pv[:, 22, :], in0=pv[:, 20, :], in1=pv[:, 1, :], op=ALU.mult))
            link(tt(out=pv[:, 21, :], in0=pv[:, 21, :], in1=pv[:, 22, :], op=ALU.subtract))
            link(tt(out=pv[:, 19, :], in0=pv[:, 21, :], in1=pv[:, 14, :], op=ALU.mult))
            dve.sem_inc(s_pow, 1)
            dve.wait_ge(s_win, 16)
            dve.wait_ge(s_gm, 16)
            for k in range(DC):
                ts(w_in_sb[:, k, :], w_in_sb[:, k, :], M4[:, 0, 0, k:k + 1], None, ALU.mult).then_inc(s_wing, 1)
            dve.wait_ge(s_pt, 1)
            link(nc.vector.tensor_copy(cf, AX2[0][:, 0:128].rearrange("p (v q) -> p v q", v=4)))
            for r in range(2):
                dve.wait_ge(s_ct, r + 1)
                src = (AX2[1] if r == 0 else UP[1])[:, 0:BK]
                link(nc.vector.tensor_copy(Cs[:, r], src.rearrange("p (q c) -> p q c", q=PR)))
                dve.sem_inc(s_cc, 1)
            link(nc.vector.memset(E[:, 0, :, 0], 1.0))
            link(nc.vector.memset(E[:, 1, :, 0], 0.0))
            link(nc.vector.tensor_copy(E[:, :, :, 1], cf[:, 0:2, :]))

            def cmul(re, im, ar, ai, br, bi, t0, t1, neg_im=False):
                link(tt(out=t0, in0=ar, in1=br, op=ALU.mult))
                link(tt(out=t1, in0=ai, in1=bi, op=ALU.mult))
                link(tt(out=re, in0=t0, in1=t1, op=ALU.subtract))
                link(tt(out=t0, in0=ar, in1=bi, op=ALU.mult))
                link(tt(out=t1, in0=ai, in1=br, op=ALU.mult))
                if neg_im:
                    link(nc.vector.scalar_tensor_tensor(out=im, in0=t0, scalar=-1.0, in1=t1, op0=ALU.mult, op1=ALU.subtract))
                else:
                    link(tt(out=im, in0=t0, in1=t1, op=ALU.add))

            for j in range(2, TAU + 1):
                cmul(E[:, 0, :, j], E[:, 1, :, j], E[:, 0, :, j - 1], E[:, 1, :, j - 1], cf[:, 0, :], cf[:, 1, :],
                     tw[:, 0:PR], tz[:, 0:PR])
            for t in range(TAU):
                link(nc.vector.tensor_copy(Er[:, :, :, t], E[:, :, :, TAU - 1 - t]))
            link(nc.vector.tensor_copy(A4[:, 0, 0, :], E[:, 0, :, TAU]))
            link(nc.vector.tensor_copy(A4[:, 1, 1, :], E[:, 0, :, TAU]))
            link(nc.vector.tensor_copy(A4[:, 1, 0, :], E[:, 1, :, TAU]))
            link(ts(A4[:, 0, 1, :], E[:, 1, :, TAU], -1.0, None, ALU.mult))
            dve.wait_ge(s_bc, 16 * 5)
            gb = lambda r: cf[:, 2 + r, :].unsqueeze(2).broadcast_to([P, PR, C])
            v16 = lambda t: t[:, 0:PR * C].rearrange("p (q c) -> p q c", q=PR)
            cmul(Bb[:, 0], Bb[:, 1], gb(0), gb(1), Braw[:, 0], Braw[:, 1], v16(tw), v16(tz))
            for q in range(0, PR, 8):
                e = lambda r: Er[:, r, q:q + 8, :].unsqueeze(3).broadcast_to([P, 8, TAU, C])
                bb = lambda r: Bb[:, r, q:q + 8, :].unsqueeze(2).broadcast_to([P, 8, TAU, C])
                v = lambda t: t[:, 0:1024].rearrange("p (q t c) -> p q t c", q=8, t=TAU)
                cmul(Wst[:, 0, q:q + 8], Wst[:, 1, q:q + 8], e(0), e(1), bb(0), bb(1), v(tw), v(tz))
                dve.sem_inc(s_Wr, 1)
            for q in range(0, PR, 8):
                e = lambda r: E[:, r, q:q + 8, :].unsqueeze(3).broadcast_to([P, 8, TAU + 1, C])
                cc = lambda r: Cs[:, r, q:q + 8, :].unsqueeze(2).broadcast_to([P, 8, TAU + 1, C])
                v = lambda t: t[:, 0:1152].rearrange("p (q t c) -> p q t c", q=8, t=TAU + 1)
                cmul(Gst[:, 0, q:q + 8], Gst[:, 1, q:q + 8], e(0), e(1), cc(0), cc(1), v(tw), v(tz), neg_im=True)
            dve.sem_inc(s_Gr, 2)
            dve.wait_ge(s_tz, 16 * 8)
            link(tt(out=dstep, in0=ident[0:C, 0:C].unsqueeze(1).broadcast_to([C, G, C]),
                    in1=Dc.unsqueeze(2).broadcast_to([C, G, C]), op=ALU.mult))
            for q in range(16):
                dve.wait_ge(s_kr, q + 1)
                nc.vector.tensor_copy(KR[:, same_rows(q), :],
                                      AX2[q % 2][0:C, :].rearrange("c (g m) -> c g m", g=4)).then_inc(s_kc, 1)
            dve.wait_ge(s_kc, 16)
            tt(out=KR[:, :, 0:C], in0=KR[:, :, 0:C], in1=dstep, op=ALU.add).then_inc(s_krd, 1)

            def copy_U(K):
                for q in range(0, 16, 2):
                    dve.wait_ge(s_ut, 16 * K + q + 1)
                    nc.vector.tensor_copy(U[K][:, BK * q:BK * q + BK], AX2[q % 2][:, :]).then_inc(s_uv, 1)

            def copy_states_re(K):
                if K == 1:
                    dve.wait_ge(s_y, 16)
                    link(nc.vector.tensor_copy(St[:, :, :, 0], St[:, :, :, 128]))
                else:
                    dve.wait_ge(s_gd, 32)
                    dve.wait_ge(s_kr, 16)
                    link(nc.vector.memset(St[:, :, :, 0], 0.0))
                dve.sem_inc(s_s0, 1)
                for q in range(16):
                    dve.wait_ge(s_v, 16 * K + q + 1)
                    ps = AX2[q % 2][0:N, :].rearrange("n (q a k) -> n q a k", q=2, a=2)
                    for a in range(2):
                        last = nc.vector.tensor_copy(St[N * a:N * a + N, 0, 2 * q:2 * q + 2, 1:129], ps[:, :, a, :])
                    last.then_inc(s_vr, 1)

            def scan(K, part):
                if part == 0:
                    dve.wait_ge(s_vr, 16 * (K + 1))
                    dve.wait_ge(s_vi, 16 * (K + 1))
                base = 3 * (128 * K + 16 * part)
                STEPS = 8
                with dve.Fori(0, 16 // STEPS) as j:
                    for c in range(STEPS):
                        k = STEPS * j + (16 * part + c)
                        n = 3 * STEPS * j + (base + 3 * c)
                        old = St[:, :, :, bass.ds(k, 1)].rearrange("p r q o -> p r (q o)")
                        new = St[:, :, :, bass.ds(k + 1, 1)].rearrange("p r q o -> p r (q o)")
                        tt(out=M4[:, :, :, :], in0=A4[:, :, :, :], in1=old.unsqueeze(1).broadcast_to([P, 2, 2, PR]),
                           op=ALU.mult).then_inc(s_sc, 1)
                        dve.wait_ge(s_sc, n + 1)
                        tt(out=T2, in0=M4[:, :, 0, :], in1=M4[:, :, 1, :], op=ALU.add).then_inc(s_sc, 1)
                        dve.wait_ge(s_sc, n + 2)
                        tt(out=new, in0=new, in1=T2, op=ALU.add).then_inc(s_sc, 1)
                        dve.wait_ge(s_sc, n + 3)
                if part == 7:
                    dve.sem_inc(s_scd, 1)

            copy_U(0)
            copy_states_re(0)
            for part in range(8):
                scan(0, part)
            copy_U(1)

            def gate_tile(i):
                h = xn[i % 2]
                for nh in range(2):
                    f = slice(BK * nh, BK * nh + BK)
                    dve.wait_ge(s_th, 2 * i + nh + 1)
                    nc.vector.scalar_tensor_tensor(out=sg[:, f], in0=sg[:, f], scalar=1.0, in1=UP[nh][:, 0:BK],
                                                   op0=ALU.add, op1=ALU.mult).then_inc(s_g1, 1)
                for nh in range(2):
                    f = slice(BK * nh, BK * nh + BK)
                    dve.wait_ge(s_g1, 2 * i + nh + 1)
                    if nh == 0:
                        dve.wait_ge(s_x2[i % 2], 16 * (i // 2 + 1))
                        if i >= 2:
                            dve.wait_ge(s_hd[i % 2], 16 * (i // 2))
                    nc.vector.scalar_tensor_tensor(out=h[:, f], in0=sg[:, f], scalar=0.5, in1=xt[i % 2][:, f],
                                                   op0=ALU.mult, op1=ALU.add).then_inc(s_hh, 1)
                dve.wait_ge(s_rs2, 2 * i + 2)
                dve.wait_ge(s_gf, 16 * (i // TAU + 1))
                if i >= 1:
                    dve.wait_ge(s_hnd, 16 * i)
                    dve.wait_ge(s_ht, i)
                nc.vector.scalar_tensor_tensor(out=hn2, in0=h, scalar=rstd2[:, i:i + 1], in1=gB,
                                               op0=ALU.mult, op1=ALU.mult).then_inc(s_hn, 1)

            copy_states_re(1)
            for i in range(NT):
                if i < TAU:
                    scan(1, i)
                gate_tile(i)

            red = nc.vector.tensor_reduce
            stt = nc.vector.scalar_tensor_tensor
            dve.wait_ge(s_lc, NT)
            dve.wait_ge(s_tri, 5)
            dve.wait_ge(s_zt, NT)
            dve.wait_ge(s_sq2, NT)
            bc = lambda ap, shape: ap.unsqueeze(len(ap.shape)).broadcast_to(shape)
            link(nc.vector.tensor_copy(iof, ioi))
            link(nc.vector.tensor_copy(tidf.rearrange("p i j -> p (i j)"), tid))
            link(nc.vector.tensor_copy(zf, zi))
            gl, el = LG[:, :, 0:GR], LG[:, :, GR:GR + NE].rearrange("p i (g j) -> p i g j", g=GR)

            def first_max(oh, v, m, cand, n):
                link(red(m, v, AX.X, ALU.max))
                link(tt(out=oh, in0=v, in1=bc(m, [P, NT, n]), op=ALU.is_ge))
                link(stt(out=cand, in0=oh, scalar=-64.0, in1=iof[:, 0:n].unsqueeze(1).broadcast_to([P, NT, n]),
                         op0=ALU.mult, op1=ALU.add))
                link(red(rt_mn, cand, AX.X, ALU.min))
                link(tt(out=oh, in0=cand, in1=bc(rt_mn, [P, NT, n]), op=ALU.is_equal))

            first_max(rt_og, gl, rt_gm, rt_c[:, :, 0:GR], GR)
            link(tt(out=rt_d, in0=gl, in1=bc(rt_gm, [P, NT, GR]), op=ALU.subtract))
            dve.sem_inc(s_rt, 1)
            link(tt(out=rt_e4, in0=el.rearrange("p i g j -> p i j g"), in1=rt_og.unsqueeze(2).broadcast_to([P, NT, EG, GR]),
                    op=ALU.mult))
            link(red(rt_ein, rt_e4, AX.X, ALU.add))
            first_max(rt_o1, rt_ein, rt_m1, rt_c, EG)
            link(stt(out=rt_ein, in0=rt_o1, scalar=-BIG, in1=rt_ein, op0=ALU.mult, op1=ALU.add))
            first_max(rt_o2, rt_ein, rt_m2, rt_c, EG)
            link(tt(out=rt_x, in0=rt_m2, in1=rt_m1, op=ALU.subtract))
            dve.sem_inc(s_rt, 1)
            dve.wait_ge(s_re, 2)
            link(red(rt_gm, rt_d, AX.X, ALU.add))
            link(nc.vector.reciprocal(rt_gm, rt_gm))
            link(ts(rt_m1, rt_x, 1.0, None, ALU.add))
            link(nc.vector.reciprocal(rt_m1, rt_m1))
            link(tt(out=gates[:, :, 0], in0=rt_gm, in1=rt_m1, op=ALU.mult))
            link(tt(out=gates[:, :, 1], in0=gates[:, :, 0], in1=rt_x, op=ALU.mult))
            for mm, oo in ((rt_M1, rt_o1), (rt_M2, rt_o2)):
                for g in range(GR):
                    link(tt(out=mm[:, :, EG * g:EG * g + EG], in0=oo, in1=rt_og[:, :, g:g + 1].broadcast_to([P, NT, EG]),
                            op=ALU.mult))
            link(tt(out=rt_M, in0=rt_M1, in1=rt_M2, op=ALU.add))
            dve.sem_inc(s_rt, 1)
            link(nc.vector.memset(rt_P[:, 0, :], 0.0))
            for i in range(1, NT):
                link(tt(out=rt_P[:, i, :], in0=rt_P[:, i - 1, :], in1=rt_M[:, i - 1, :], op=ALU.add))
            link(tt(out=rt_tot, in0=rt_P[:, NT - 1, :], in1=rt_M[:, NT - 1, :], op=ALU.add))
            dve.sem_inc(s_rt, 1)
            dve.wait_ge(s_rk, 1)
            link(ts(rt_ci, AX2[1][:, 0:NE], 127.0, None, ALU.add))
            link(ts(rt_ci, rt_ci, 7, None, ALU.arith_shift_right))
            link(ts(rt_nb, rt_ci, 1.0, None, ALU.max))
            link(nc.vector.memset(rt_one, 1.0))
            link(nc.vector.tensor_tensor_scan(rt_be, rt_one, rt_nb, 0.0, ALU.mult, ALU.add))
            link(tt(out=rt_bs, in0=rt_be, in1=rt_nb, op=ALU.subtract))
            link(stt(out=rt_S, in0=rt_bs.unsqueeze(1).broadcast_to([P, NT, NE]), scalar=128.0,
                     in1=AX2[0][:, :].rearrange("p (i e) -> p i e", i=NT), op0=ALU.mult, op1=ALU.add))
            for j, mm in enumerate((rt_M1, rt_M2)):
                link(tt(out=mm, in0=mm, in1=rt_S, op=ALU.mult))
                link(red(rt_sf[:, :, j], mm, AX.X, ALU.add))
            link(nc.vector.tensor_copy(slots, rt_sf))
            link(ts(rt_lo, slots, P - 1, None, ALU.bitwise_and))
            link(ts(rt_hi, slots, 7, None, ALU.arith_shift_right))
            link(nc.vector.tensor_copy(lof, rt_lo))
            link(nc.vector.tensor_copy(hif, rt_hi))
            ramp = lambda n: iof[:, 0:n].unsqueeze(1).broadcast_to([P, 2 * NT, n])
            flat = lambda ap: ap.rearrange("p i j -> p (i j)")
            rows_p, rows_b = (v.rearrange("p i j m -> p (i j) m") for v in (ohP, ohB))
            link(tt(out=rows_p, in0=bc(flat(lof), [P, 2 * NT, P]), in1=ramp(P), op=ALU.is_equal))
            link(tt(out=rows_b, in0=bc(flat(hif), [P, 2 * NT, NBT]), in1=ramp(NBT), op=ALU.is_equal))
            link(tt(out=rows_b, in0=rows_b, in1=bc(flat(tidf), [P, 2 * NT, NBT]), op=ALU.mult))
            dve.sem_inc(s_rt, 1)
            one = slice(0, 1)
            be, bl = rt_be[one], rt_bk[one]
            link(tt(out=bl, in0=be.unsqueeze(1).broadcast_to([1, NBT, NE]),
                    in1=iof[one, 0:NBT].unsqueeze(2).broadcast_to([1, NBT, NE]), op=ALU.is_le))
            link(red(rt_eb[one, 0, :], bl, AX.X, ALU.add))
            link(tt(out=bl, in0=be.unsqueeze(1).broadcast_to([1, NBT, NE]),
                    in1=iof[one, 1:NBT + 1].unsqueeze(2).broadcast_to([1, NBT, NE]), op=ALU.is_equal))
            link(red(rt_eb[one, 1, :], bl[:, :, 0:NE - 1], AX.X, ALU.add))
            link(red(rt_eb[one, 2, :], bl[:, :, 0:NE - 2], AX.X, ALU.add))
            link(ts(rt_eb[one, 0, :], rt_eb[one, 0, :], float(NE - 1), None, ALU.min))
            link(nc.vector.tensor_copy(blk[:, 0:3 * NBT].rearrange("o (v b) -> o v b", v=3), rt_eb[one]))
            link(nc.vector.tensor_scalar(blk[:, 3 * NBT:3 * NBT + 1], be[:, NE - 1:NE], 1.0, None, ALU.subtract))
            dve.wait_ge(s_tb, 1)
            link(stt(out=free, in0=AX2[1][:, 0:NBT], scalar=0.5, in1=zf, op0=ALU.is_lt, op1=ALU.mult))
            link(stt(out=rows, in0=AX2[1][:, 0:NBT], scalar=-1.0, in1=free, op0=ALU.add, op1=ALU.add))

        @block.tensor
        def _(pe):
            pe.wait_ge(s_ident, 3)

            def transpose_x(i):
                pe.wait_ge(s_xn, i + 1)
                if i >= 1:
                    pe.wait_ge(s_hT, i)
                for k in range(DC):
                    last = nc.tensor.transpose(TP[:, P * k:P * k + P], xn[i % 2][:, P * k:P * k + P], ident[:, :])
                last.then_inc(s_tp, 1)

            def product_u(i):
                pe.wait_ge(s_hT, i + 1)
                if i == 0:
                    pe.wait_ge(s_wing, DC)
                if i >= 2:
                    pe.wait_ge(s_ue, i - 1)
                for k in range(DC):
                    for nh in range(2):
                        last = nc.tensor.matmul(UP[i % 2][:, BK * nh:BK * nh + BK], hT[i % 2][:, P * k:P * k + P],
                                                w_in_sb[:, k, BK * nh:BK * nh + BK], start=(k == 0), stop=(k == DC - 1))
                last.then_inc(s_mm, 1)

            def transpose_u(K):
                pe.wait_ge(s_ue, TAU * (K + 1))
                for q in range(16):
                    if q >= 2:
                        if q % 2 == 0:
                            pe.wait_ge(s_uv, 8 * K + q // 2)
                        else:
                            pe.wait_ge(s_ua, 8 * K + q // 2)
                    for g in range(4 * q, 4 * q + 4):
                        last = nc.tensor.transpose(AX2[q % 2][:, P * (g % 4):P * (g % 4) + P],
                                                   R2[:, P * g:P * g + P], ident[:, :])
                    last.then_inc(s_ut, 1)

            def collect(K):
                if K == 1:
                    pe.wait_ge(s_z, 16)
                pe.wait_ge(s_uv, 8 * K + 8)
                pe.wait_ge(s_ua, 8 * K + 8)
                for q in range(16):
                    b = q // 2
                    if q % 2 == 0:
                        pe.wait_ge(s_wl[b % 2], 16 * (4 * K + b // 2 + 1))
                    if q >= 2:
                        pe.wait_ge(s_vr, 16 * K + q - 1)
                        pe.wait_ge(s_vi, 16 * K + q - 1)
                    for g in range(4 * q, 4 * q + 4):
                        last = nc.tensor.matmul(AX2[q % 2][:, P * (g % 4):P * (g % 4) + P],
                                                wb[b % 2][:, P * (g % 8):P * (g % 8) + P],
                                                U[K][:, P * g:P * g + P], start=True, stop=True)
                    last.then_inc(s_v, 1)

            pe.wait_ge(s_pow, 1)
            for j, v in enumerate((16, 17, 18, 19)):
                last = nc.tensor.transpose(AX2[0][:, PR * j:PR * j + PR], pv[:, v, :], ident[0:PR, 0:PR])
            last.then_inc(s_pt, 1)
            pe.wait_ge(s_c, 16 * 16)
            for r in range(2):
                dst = AX2[1] if r == 0 else UP[1]
                for t in range(4):
                    last = nc.tensor.transpose(dst[:, P * t:P * t + P], Cn[:, r, t, :], ident[:, :])
                last.then_inc(s_ct, 1)
            transpose_x(0)
            pe.wait_ge(s_cc, 2)

            for i in range(TAU):
                transpose_x(i + 1)
                product_u(i)
            for q in range(16):
                pe.wait_ge(s_Wr, (2 * q + 1) // 8 + 1)
                if q >= 2:
                    pe.wait_ge(s_wc, 2 * (q - 1))
                for l in range(2):
                    for r in range(2):
                        last = nc.tensor.transpose(AX2[q % 2][:, 256 * l + P * r:256 * l + P * r + P],
                                                   Wst[:, r, 2 * q + l].rearrange("p t c -> p (t c)"), ident[:, :])
                last.then_inc(s_wt, 1)
            pe.wait_ge(s_Gr, 2)
            pe.wait_ge(s_wc, 32)
            for q in range(16):
                if q >= 2:
                    pe.wait_ge(s_kc, q - 1)
                rows = slice(N * (q % 2), N * (q % 2) + N)
                for l in range(4):
                    pr = 4 * (q // 2) + l
                    for r in range(2):
                        last = nc.tensor.matmul(AX2[q % 2][0:C, P * l:P * l + P], Bb[rows, r, pr, :],
                                                Gst[rows, r, pr, 0:TAU, :].rearrange("p j c -> p (j c)"),
                                                start=(r == 0), stop=(r == 1))
                last.then_inc(s_kr, 1)
            pe.wait_ge(s_krd, 1)
            transpose_u(0)
            collect(0)
            for i in range(TAU, NT):
                if i + 1 < NT:
                    transpose_x(i + 1)
                product_u(i)
            pe.wait_ge(s_vr, 16)
            pe.wait_ge(s_vi, 16)
            pe.wait_ge(s_td, 16 * 8)
            transpose_u(1)

            def read_out(K):
                pe.wait_ge(s_uv, 16)
                pe.wait_ge(s_ua, 16)
                pe.wait_ge(s_scd, K + 1)
                if K == 1:
                    pe.wait_ge(s_lc, TAU)
                for q in range(16):
                    b = q // 2
                    if q % 2 == 0:
                        pe.wait_ge(s_tg[b % 2], 48 * (4 * K + b // 2 + 1))
                    if q >= 2:
                        pe.wait_ge(s_z, 16 * K + q - 1)
                    t = tgb[b % 2]
                    gg = t[:, 1024:2048].rearrange("p (r q x) -> p r q x", r=2, q=4)
                    a = q % 2
                    rows = slice(N * a, N * a + N)
                    for l in range(4):
                        g = 8 * b + 2 * l + a
                        nc.tensor.matmul(AX2[a][:, P * l:P * l + P], U[K][:, P * g:P * g + P],
                                         t[:, P * (g % 8):P * (g % 8) + P], start=(l == 0), stop=False,
                                         skip_group_check=True)
                    for l in range(4):
                        for r in range(2):
                            last = nc.tensor.matmul(AX2[a][:, P * l:P * l + P], St[rows, r, 4 * b + l, 0:128],
                                                    gg[rows, r, l, :], start=False, stop=(r == 1),
                                                    skip_group_check=True)
                    last.then_inc(s_y, 1)

            def transpose_z(i):
                pe.wait_ge(s_z, 16 * (i // TAU + 1))
                if i % TAU == 0:
                    pe.wait_ge(s_hc, i)
                    pe.wait_ge(s_hT, NT)
                else:
                    pe.wait_ge(s_zc, i)
                    if i >= 2:
                        pe.wait_ge(s_hc, i - 1)
                for k in range(DC):
                    last = nc.tensor.transpose(TP[:, P * k:P * k + P],
                                               R2[:, D * (i % TAU) + P * k:D * (i % TAU) + P * k + P], ident[:, :])
                last.then_inc(s_zt, 1)

            def product_vg(i, nh, ks):
                if i == 0:
                    pe.wait_ge(s_wo, 32)
                    pe.wait_ge(s_ue, NT)
                if i >= 1:
                    pe.wait_ge(s_g1, 2 * (i - 1) + nh + 1)
                for k in ks:
                    w = (R1 if k < 4 else R3)[:, 2048 * (k % 4):2048 * (k % 4) + 2048]
                    for vg in range(2):
                        last = nc.tensor.matmul(UP[nh][:, BK * vg:BK * vg + BK], hT[i % 2][:, P * k:P * k + P],
                                                w[:, D * vg + BK * nh:D * vg + BK * nh + BK],
                                                start=(k == 0), stop=(k == DC - 1))
                if k == DC - 1:
                    last.then_inc(s_vg, 1)

            def transpose_hn(i):
                pe.wait_ge(s_hn, i + 1)
                pe.wait_ge(s_zc, min(i + 2, TAU * (i // TAU) + TAU))
                for k in range(DC):
                    last = nc.tensor.transpose(TP[:, P * k:P * k + P], hn2[:, P * k:P * k + P], ident[:, :])
                last.then_inc(s_ht, 1)

            def router(i):
                pe.wait_ge(s_hc, i + 1)
                if i == 0:
                    pe.wait_ge(s_wrl, 32)
                    pe.wait_ge(s_vr, 32)
                    pe.wait_ge(s_vi, 32)
                if i == TAU:
                    pe.wait_ge(s_z, 32)
                if i >= 1:
                    pe.wait_ge(s_lc, i)
                for k in range(DC):
                    last = nc.tensor.matmul(AX2[0][:, 0:GR + NE], hn2T[:, P * k:P * k + P], wr[:, k, :],
                                            start=(k == 0), stop=(k == DC - 1))
                last.then_inc(s_lg, 1)

            for K in range(2):
                read_out(K)
                if K == 0:
                    pe.wait_ge(s_s0, 2)
                    collect(1)
                t0 = TAU * K
                transpose_z(t0)
                for i in range(t0, t0 + TAU):
                    pe.wait_ge(s_zc, i + 1)
                    product_vg(i, 0, range(DC))
                    if i > t0:
                        transpose_hn(i - 1)
                    product_vg(i, 1, range(4))
                    if i > t0:
                        router(i - 1)
                    if i + 1 < t0 + TAU:
                        transpose_z(i + 1)
                    product_vg(i, 1, range(4, DC))
                transpose_hn(t0 + TAU - 1)
                router(t0 + TAU - 1)

            pe.wait_ge(s_rt, 4)
            pe.wait_ge(s_tri, 5)
            pe.wait_ge(s_lc, NT)
            nc.tensor.matmul(AX2[0][:, :], tri, rt_M.rearrange("p i e -> p (i e)"), start=True, stop=False)
            nc.tensor.matmul(AX2[0][:, :], ones, rt_P.rearrange("p i e -> p (i e)"), start=False, stop=True)
            nc.tensor.matmul(AX2[1][:, 0:NE], ones, rt_tot, start=True, stop=True).then_inc(s_rk, 1)
            pe.wait_ge(s_rt, 5)
            for i in range(NT):
                for j in range(2):
                    last = nc.tensor.matmul(AX2[1][:, 0:NBT], ohP[:, i, j, :], ohB[:, i, j, :],
                                            start=(i + j == 0), stop=(i == NT - 1 and j == 1))
            last.then_inc(s_tb, 1)


def build_experts(nc, w1, w3, w2, hn_d, y_d, ident, rows, blk):
    RAW, RING, NPC, PC = 3, 8, 6, 2048
    ctx = ExitStack()
    with ctx:
        def sb(name, shape, dt=F32):
            return ctx.enter_context(nc.sbuf_tensor(name, shape, dt))

        def sem(name):
            return ctx.enter_context(nc.semaphore(name))

        raw = [sb(f"raw{j}", [P, PC]) for j in range(RAW)]
        wH = sb("wH", [P, RING * PC], F32R)
        wL = sb("wL", [P, RING * PC], F32R)
        xg = [sb(f"xg{j}", [P, D]) for j in range(2)]
        xH = [sb(f"xH{j}", [P, D], F32R) for j in range(2)]
        xL = [sb(f"xL{j}", [P, D], F32R) for j in range(2)]
        token = sb("token", [P, NBT], I32)
        idx = [sb(f"idx{j}", [P, 1], I32) for j in range(2)]
        odx = [sb(f"odx{j}", [P, 1], I32) for j in range(2)]
        after = sb("after", [1, 1])
        sil = sb("sil", [P, FF])
        hm = sb("hm", [P, FF])
        hH = sb("hH", [P, FF], F32R)
        hL = sb("hL", [P, FF], F32R)
        yo = [sb(f"yo{j}", [P, D]) for j in range(2)]
        XB = ctx.enter_context(nc.psum_tensor("XB", [P, BK], F32))
        HB = ctx.enter_context(nc.psum_tensor("HB", [P, BK], F32))
        H13 = [ctx.enter_context(nc.psum_tensor(f"H13_{j}", [P, 2 * BK], F32)) for j in range(2)]
        YB = ctx.enter_context(nc.psum_tensor("YB", [P, 2 * BK], F32))

        s_raw = [sem(f"piece_loaded{j}") for j in range(RAW)]
        s_pH = sem("pieces_high")
        s_pL = sem("pieces_split")
        s_xg = [sem(f"rows_gathered{j}") for j in range(2)]
        s_tok = sem("tokens_ready")
        s_idx = sem("indices_ready")
        s_odx = sem("y_indices_ready")
        s_xt = sem("rows_transposed")
        s_xH = sem("rowsT_high")
        s_xL = sem("rowsT_split")
        s_1 = sem("first_product")
        s_sil = sem("silu_ready")
        s_hm = sem("hidden_ready")
        s_ht = sem("hidden_transposed")
        s_hH = sem("hiddenT_high")
        s_hL = sem("hiddenT_split")
        s_2 = sem("second_product")
        s_yA = sem("y_copied_act")
        s_yV = sem("y_copied_dve")
        s_ys = [sem(f"y_stored{j}") for j in range(2)]

        block = ctx.enter_context(nc.Block())
        word = lambda eng, j, hi: eng.value_load(blk[0:1, bass.ds(j, 1)], min_val=0, max_val=hi)
        last_block = lambda eng: eng.value_load(blk[0:1, 3 * NBT:3 * NBT + 1], min_val=0, max_val=NB - 1)

        @block.sync
        def _(sp):
            def load(e, j):
                row = bass.ds(e, 1)
                dst = raw[j % RAW][:, :].rearrange("p (k n) -> p k n", k=2)
                if j < 4:
                    for half, w in enumerate((w1, w3)):
                        src = w.rearrange("e (k p) f -> p e k f", p=P)[:, row, 2 * j:2 * j + 2, :]
                        sp.dma_start(dst[:, :, FF * half:FF * half + FF],
                                     src.rearrange("p e k f -> p (e k) f")).then_inc(s_raw[j % RAW], 16)
                else:
                    for half in range(2):
                        kt = 2 * (j - 4) + half
                        src = w2.rearrange("e (k p) f -> p e k f", p=P)[:, row, kt, :]
                        sp.dma_start(dst[:, half, :], src.rearrange("p e f -> p (e f)")).then_inc(s_raw[j % RAW], 16)

            for j in range(NPC):
                if j >= RAW:
                    sp.wait_ge(s_pL, j + 1 - RAW)
                load(0, j)
            with sp.Fori(0, NE - 1) as i:
                for j in range(NPC):
                    sp.wait_ge(s_pL, NPC * i + (NPC + j + 1 - RAW))
                    load(i + 1, j)

        @block.gpsimd
        def _(pool):
            def gather(x, j, later):
                if later:
                    pool.wait_ge(s_xt, 2 * x - 2)
                nc.gpsimd.tensor_copy(idx[j][:, :], token[:, bass.ds(x, 1)]).then_inc(s_idx, 1)
                pool.wait_ge(s_idx, x + 1)
                nc.gpsimd.tensor_tensor(out=after[:, :], in0=ident[0:1, 0:1], in1=ident[0:1, 0:1], op=ALU.add)
                pool.indirect_dma_start(out=xg[j][:, :], out_offset=None, in_=hn_d,
                                        in_offset=bass.IndirectOffsetOnAxis(ap=idx[j][:, :], axis=0)
                                        ).then_inc(s_xg[j], 16)

            def scatter(y, j):
                pool.wait_ge(s_yA, y + 1)
                pool.wait_ge(s_yV, y + 1)
                nc.gpsimd.tensor_copy(odx[j][:, :], rows[:, bass.ds(y, 1)]).then_inc(s_odx, 1)
                pool.wait_ge(s_odx, y + 1)
                nc.gpsimd.tensor_tensor(out=after[:, :], in0=ident[0:1, 0:1], in1=ident[0:1, 0:1], op=ALU.add)
                pool.indirect_dma_start(out=y_d, out_offset=bass.IndirectOffsetOnAxis(ap=odx[j][:, :], axis=0),
                                        in_=yo[j][:, :], in_offset=None).then_inc(s_ys[j], 16)

            pool.wait_ge(s_tok, 1)
            gather(0, 0, False)
            gather(1, 1, False)
            last = last_block(pool)
            with pool.Fori(0, NB // 2) as i:
                for j in range(2):
                    with pool.If(2 * i + j < last + 1):
                        gather(2 * i + j + 2, j, True)
                        scatter(2 * i + j, j)
                        pool.nop()
            pool.wait_ge(s_ys[0], 16 * ((last + 2) // 2))
            pool.wait_ge(s_ys[1], 16 * ((last + 1) // 2))
            for j in range(2):
                pool.wait_ge(s_xg[j], 16)

        @block.scalar
        def _(act):
            def high(e, j):
                act.wait_ge(s_raw[j % RAW], 32 * (2 * e + j // RAW + 1))
                slot = (NPC * e + j) % RING
                out = wH[:, bass.ds(slot * PC, PC)] if not isinstance(slot, int) else wH[:, slot * PC:slot * PC + PC]
                nc.scalar.activation(out, raw[j % RAW][:, :], ACT.Copy).then_inc(s_pH, 1)

            def rows_high(x, j, half, later):
                act.wait_ge(s_xt, 2 * x + half + 1)
                if later:
                    act.wait_ge(s_1, x - 1)
                nc.scalar.activation(xH[j][:, BK * half:BK * half + BK], XB[:, :], ACT.Copy).then_inc(s_xH, 1)

            def hidden_high(y):
                act.wait_ge(s_ht, y + 1)
                act.wait_ge(s_2, y)
                nc.scalar.activation(hH[:, :], HB[:, :], ACT.Copy).then_inc(s_hH, 1)

            def silu(g, j):
                act.wait_ge(s_1, g + 1)
                act.wait_ge(s_hm, g)
                nc.scalar.activation(sil[:, :], H13[j][:, 0:BK], ACT.Silu).then_inc(s_sil, 1)

            def copy_y(y, j):
                act.wait_ge(s_2, y + 1)
                act.wait_ge(s_ys[j], 16 * (y // 2))
                nc.scalar.activation(yo[j][:, 0:BK], YB[:, 0:BK], ACT.Copy).then_inc(s_yA, 1)

            for j in range(NPC):
                high(0, j)
                if j == 1:
                    for half in range(2):
                        rows_high(0, 0, half, False)
            for j in range(2):
                high(1, j)

            def step(g, j, peeled):
                e = word(act, g, NE - 1)
                last = word(act, NBT + g, 1)
                if not peeled:
                    new = word(act, NBT + g - 1, 1)
                    freed = word(act, 2 * NBT + g - 1, 1)
                    hidden_high(g - 1)
                    with act.If(new > 0):
                        high(e, 3)
                        act.nop()
                rows_high(g + 1, 1 - j, 0, not peeled)
                if not peeled:
                    with act.If(new > 0):
                        high(e, 4)
                        high(e, 5)
                        act.nop()
                    copy_y(g - 1, 1 - j)
                rows_high(g + 1, 1 - j, 1, not peeled)
                if not peeled:
                    before = word(act, g - 1, NE - 1)
                    with act.If(freed > 0):
                        high(before + 2, 0)
                        high(before + 2, 1)
                        act.nop()
                silu(g, j)
                with act.If(last > 0):
                    high(e + 1, 2)
                    act.nop()

            step(0, 0, True)
            last = last_block(act)
            with act.Fori(0, NB // 2) as i:
                for j in range(2):
                    with act.If(2 * i + j < last):
                        step(2 * i + j + 1, 1 - j, False)
                        act.nop()
            hidden_high(last)
            act.wait_ge(s_2, last + 1)
            for j in range(2):
                act.wait_ge(s_ys[j], 16 * (last // 2))
            with act.If(last % 2 < 1):
                nc.scalar.activation(yo[0][:, 0:BK], YB[:, 0:BK], ACT.Copy).then_inc(s_yA, 1)
            with act.Else():
                nc.scalar.activation(yo[1][:, 0:BK], YB[:, 0:BK], ACT.Copy).then_inc(s_yA, 1)

        @block.vector
        def _(dve):
            sub = lambda out, a, h: nc.vector.tensor_tensor(out=out, in0=a, in1=h.bitcast(F32), op=ALU.subtract)

            def low(e, j):
                dve.wait_ge(s_pH, NPC * e + j + 1)
                slot = (NPC * e + j) % RING
                at = bass.ds(slot * PC, PC) if not isinstance(slot, int) else slice(slot * PC, slot * PC + PC)
                sub(wL[:, at], raw[j % RAW][:, :], wH[:, at]).then_inc(s_pL, 1)

            def rows_low(x, j, half):
                dve.wait_ge(s_xH, 2 * x + half + 1)
                f = slice(BK * half, BK * half + BK)
                sub(xL[j][:, f], XB[:, :], xH[j][:, f]).then_inc(s_xL, 1)

            def hidden_low(y):
                dve.wait_ge(s_hH, y + 1)
                sub(hL[:, :], HB[:, :], hH[:, :]).then_inc(s_hL, 1)

            def hidden(g, j):
                dve.wait_ge(s_sil, g + 1)
                dve.wait_ge(s_ht, g)
                nc.vector.tensor_tensor(out=hm[:, :], in0=sil[:, :], in1=H13[j][:, BK:2 * BK], op=ALU.mult).then_inc(s_hm, 1)

            def copy_y(y, j):
                dve.wait_ge(s_2, y + 1)
                dve.wait_ge(s_ys[j], 16 * (y // 2))
                nc.vector.tensor_copy(yo[j][:, BK:D], YB[:, BK:2 * BK]).then_inc(s_yV, 1)

            nc.vector.tensor_scalar(token[:, :], rows[:, :], S - 1, None, ALU.bitwise_and).then_inc(s_tok, 1)
            for j in range(NPC):
                low(0, j)
                if j == 1:
                    for half in range(2):
                        rows_low(0, 0, half)
            for j in range(2):
                low(1, j)

            def step(g, j, peeled):
                e = word(dve, g, NE - 1)
                last = word(dve, NBT + g, 1)
                if not peeled:
                    new = word(dve, NBT + g - 1, 1)
                    freed = word(dve, 2 * NBT + g - 1, 1)
                    hidden_low(g - 1)
                    with dve.If(new > 0):
                        low(e, 3)
                        dve.nop()
                rows_low(g + 1, 1 - j, 0)
                if not peeled:
                    with dve.If(new > 0):
                        low(e, 4)
                        low(e, 5)
                        dve.nop()
                    copy_y(g - 1, 1 - j)
                rows_low(g + 1, 1 - j, 1)
                if not peeled:
                    before = word(dve, g - 1, NE - 1)
                    with dve.If(freed > 0):
                        low(before + 2, 0)
                        low(before + 2, 1)
                        dve.nop()
                hidden(g, j)
                with dve.If(last > 0):
                    low(e + 1, 2)
                    dve.nop()

            step(0, 0, True)
            last = last_block(dve)
            with dve.Fori(0, NB // 2) as i:
                for j in range(2):
                    with dve.If(2 * i + j < last):
                        step(2 * i + j + 1, 1 - j, False)
                        dve.nop()
            hidden_low(last)
            dve.wait_ge(s_2, last + 1)
            for j in range(2):
                dve.wait_ge(s_ys[j], 16 * (last // 2))
            with dve.If(last % 2 < 1):
                nc.vector.tensor_copy(yo[0][:, BK:D], YB[:, BK:2 * BK]).then_inc(s_yV, 1)
            with dve.Else():
                nc.vector.tensor_copy(yo[1][:, BK:D], YB[:, BK:2 * BK]).then_inc(s_yV, 1)

        @block.tensor
        def _(pe):
            def transpose_rows(x, j, half):
                if half == 0:
                    pe.wait_ge(s_xg[j], 16 * (x // 2 + 1))
                if not isinstance(x, int) or 2 * x + half > 0:
                    pe.wait_ge(s_xL, 2 * x + half)
                for k in range(4):
                    f = BK * half + P * k
                    last = nc.tensor.transpose(XB[:, P * k:P * k + P], xg[j][:, f:f + P], ident[:, :])
                last.then_inc(s_xt, 1)

            def three(out, aH, aL, at, start, stop):
                nc.tensor.matmul(out, aH, wH[:, at], start=start, stop=False)
                nc.tensor.matmul(out, aH, wL[:, at], start=False, stop=False)
                return nc.tensor.matmul(out, aL, wH[:, at], start=False, stop=stop)

            def piece(e, jp):
                slot = (NPC * e + jp) % RING
                return slot * PC if isinstance(slot, int) else pe.snap(slot * PC)

            def tile(base, k, n):
                o = base + n * BK + (k % 2) * 2 * BK
                return slice(o, o + BK) if isinstance(o, int) else bass.ds(o, BK)

            def first(e, j, jp):
                pe.wait_ge(s_pL, NPC * e + jp + 1)
                base = piece(e, jp)
                for k in (2 * jp, 2 * jp + 1):
                    kk = slice(P * k, P * k + P)
                    for n in range(2):
                        last = three(H13[j][:, BK * n:BK * n + BK], xH[j][:, kk], xL[j][:, kk], tile(base, k, n),
                                     k == 0, k == DC - 1)
                return last

            def transpose_hidden(y):
                pe.wait_ge(s_hm, y + 1)
                pe.wait_ge(s_hL, y)
                for k in range(FC):
                    last = nc.tensor.transpose(HB[:, P * k:P * k + P], hm[:, P * k:P * k + P], ident[:, :])
                last.then_inc(s_ht, 1)

            def second(e, y):
                pe.wait_ge(s_hL, y + 1)
                pe.wait_ge(s_yA, y)
                pe.wait_ge(s_yV, y)
                for jp in (4, 5):
                    pe.wait_ge(s_pL, NPC * e + jp + 1)
                    base = piece(e, jp)
                    for k in (2 * jp - 8, 2 * jp - 7):
                        kk = slice(P * k, P * k + P)
                        for n in range(2):
                            last = three(YB[:, BK * n:BK * n + BK], hH[:, kk], hL[:, kk], tile(base, k, n),
                                         k == 0, k == FC - 1)
                last.then_inc(s_2, 1)

            def step(g, j, peeled):
                e = word(pe, g, NE - 1)
                if not peeled:
                    before = word(pe, g - 1, NE - 1)
                pe.wait_ge(s_xL, 2 * g + 2)
                if not isinstance(g, int):
                    pe.wait_ge(s_hm, g - 1)
                first(e, j, 0)
                if not peeled:
                    transpose_hidden(g - 1)
                first(e, j, 1)
                transpose_rows(g + 1, 1 - j, 0)
                if not peeled:
                    second(before, g - 1)
                transpose_rows(g + 1, 1 - j, 1)
                first(e, j, 2)
                first(e, j, 3).then_inc(s_1, 1)

            transpose_rows(0, 0, 0)
            transpose_rows(0, 0, 1)
            step(0, 0, True)
            last = last_block(pe)
            with pe.Fori(0, NB // 2) as i:
                for j in range(2):
                    with pe.If(2 * i + j < last):
                        step(2 * i + j + 1, 1 - j, False)
                        pe.nop()
            transpose_hidden(last)
            second(NE - 1, last)


def build_combine(nc, ln_final, h_d, y_d, out, gates):
    B = 3
    Y = 12
    ctx = ExitStack()
    with ctx:
        def sb(name, shape, dt=F32):
            return ctx.enter_context(nc.sbuf_tensor(name, shape, dt))

        def sem(name):
            return ctx.enter_context(nc.semaphore(name))

        ht = [sb(f"ht{j}", [P, D]) for j in range(NT)]
        ya = [[sb(f"y{r}_{j}", [P, D]) for r in range(2)] for j in range(Y)]
        sq = sb("sq", [P, D])
        gB = sb("gain", [P, D])
        ot = [sb(f"ot{j}", [P, D]) for j in range(B)]
        st = sb("st", [P, 2 * NT])
        mh = sb("mh", [P, 1])
        s_h = [sem(f"h_loaded{j}") for j in range(NT)]
        s_ya = [sem(f"rows_loaded{j}") for j in range(Y)]
        s_g = sem("final_gain_loaded")
        s_mh = sem("minus_half")
        s_sum = sem("sums")
        s_sq = sem("final_squares")
        s_rs = sem("final_rstd")
        s_o = sem("out_ready")
        s_od = [sem(f"out_stored{j}") for j in range(B)]
        block = ctx.enter_context(nc.Block())

        @block.sync
        def _(sp):
            def load(i):
                if i >= Y:
                    sp.wait_ge(s_sum, 2 * (i - Y) + 2)
                sp.dma_start(ht[i][:, :], tile_rows(h_d, i // TAU, i % TAU)).then_inc(s_h[i], 16)
                for r in range(2):
                    src = y_d[S * r:S * r + S]
                    sp.dma_start(ya[i % Y][r][:, :], tile_rows(src, i // TAU, i % TAU)).then_inc(s_ya[i % Y], 16)

            for i in range(NT):
                load(i)
            for j in range(B):
                sp.wait_ge(s_od[j], 16 * len(range(j, NT, B)))

        @block.gpsimd
        def _(pool):
            nc.gpsimd.memset(mh[:, :], -0.5).then_inc(s_mh, 1)
            pool.wait_ge(s_mh, 1)

            for i in range(NT):
                pool.wait_ge(s_sq, i + 1)
                nc.gpsimd.tensor_scalar(st[:, NT + i:NT + i + 1], st[:, i:i + 1], 1.0 / D, EPS, ALU.mult, ALU.add).then_inc(s_rs, 1)
                pool.wait_ge(s_rs, 2 * i + 1)
                nc.gpsimd.tensor_tensor(out=st[:, NT + i:NT + i + 1], in0=st[:, NT + i:NT + i + 1], in1=mh[:, 0:1], op=ALU.pow).then_inc(s_rs, 1)

        @block.scalar
        def _(act):
            act.dma_start(gB[:, :], ln_final.partition_broadcast(P)).then_inc(s_g, 16)

            def store(i):
                act.wait_ge(s_o, i + 1)
                act.dma_start(tile_rows(out, i // TAU, i % TAU), ot[i % B][:, :]).then_inc(s_od[i % B], 16)

            for i in range(NT):
                act.wait_ge(s_sum, 2 * i + 2)
                if i > 0:
                    act.wait_ge(s_sq, i)
                nc.scalar.activation(sq[:, :], ht[i][:, :], ACT.Square, accum_out=st[:, i:i + 1]).then_inc(s_sq, 1)
                if i >= 1:
                    store(i - 1)
            store(NT - 1)

        @block.vector
        def _(dve):
            dve.wait_ge(s_g, 16)

            def add(i):
                h = ht[i][:, :]
                dve.wait_ge(s_h[i], 16)
                dve.wait_ge(s_ya[i % Y], 32 * (i // Y + 1))
                for r in range(2):
                    nc.vector.scalar_tensor_tensor(out=h, in0=ya[i % Y][r][:, :], scalar=gates[:, i, r:r + 1], in1=h,
                                                   op0=ALU.mult, op1=ALU.add).then_inc(s_sum, 1)
                    dve.wait_ge(s_sum, 2 * i + r + 1)

            add(0)
            for i in range(NT):
                if i + 1 < NT:
                    add(i + 1)
                dve.wait_ge(s_rs, 2 * i + 2)
                if i >= B:
                    dve.wait_ge(s_od[i % B], 16 * (i // B))
                nc.vector.scalar_tensor_tensor(out=ot[i % B][:, :], in0=ht[i][:, :], scalar=st[:, NT + i:NT + i + 1],
                                               in1=gB[:, :], op0=ALU.mult, op1=ALU.mult).then_inc(s_o, 1)


def build(nc, a, out):
    W_d = nc.dram_tensor("W_d", [8 * P, 1024], F32).ap()
    T_d = nc.dram_tensor("T_d", [P, 8 * 1024], F32).ap()
    G_d = nc.dram_tensor("G_d", [2 * P, 8 * 512], F32).ap()
    h_d = nc.dram_tensor("h_d", [S, D], F32).ap()
    hn_d = nc.dram_tensor("hn_d", [S, D], F32).ap()
    y_d = nc.dram_tensor("y_d", [2 * S + P * NBT, D], F32).ap()
    with ExitStack() as ctx:
        sb = lambda name, shape, dt: ctx.enter_context(nc.sbuf_tensor(name, shape, dt))
        ident = sb("ident", [P, P], F32)
        rows = sb("rows", [P, NBT], I32)
        gates = sb("gates", [P, NT, 2], F32)
        blk = sb("blk", [1, 3 * NBT + 1], I32)
        one = lambda k: a[k][0]
        build_mixer(nc, a["x"][0], one("ln_mix"), one("ln_ffn"), one("ssm_w_in"), one("ssm_lam_re"), one("ssm_lam_im"),
                    one("ssm_log_dt"), one("ssm_b_re"), one("ssm_b_im"), one("ssm_c_re"), one("ssm_c_im"), one("ssm_d"),
                    one("ssm_w_out"), one("moe_w_group"), one("moe_w_expert"), h_d, hn_d, W_d, T_d, G_d,
                    ident, rows[:, :], gates[:, :, :], blk[:, :])
        build_experts(nc, one("moe_w1"), one("moe_w3"), one("moe_w2"), hn_d, y_d, ident, rows, blk)
        build_combine(nc, a["ln_final"], h_d, y_d, out[0], gates)


_INS = ["x", "ln_mix", "ln_ffn", "ln_final", "ssm_w_in", "ssm_lam_re", "ssm_lam_im", "ssm_log_dt", "ssm_b_re", "ssm_b_im",
        "ssm_c_re", "ssm_c_im", "ssm_d", "ssm_w_out", "moe_w_group", "moe_w_expert", "moe_w1", "moe_w3", "moe_w2"]


def kernel(**inputs):
    import numpy as _np
    import concourse.bacc as _bacc
    from concourse import mybir as _mybir
    from concourse.bass_utils import run_bass_kernel_spmd as _run

    nc = _bacc.Bacc("TRN2", target_bir_lowering=False, num_devices=1)
    arrays, aps = {}, {}
    for name in _INS:
        v = _np.ascontiguousarray(inputs[name])
        arrays[f"in_{name}"] = v
        aps[name] = nc.dram_tensor(f"in_{name}", v.shape, _mybir.dt.from_np(v.dtype), kind="ExternalInput").ap()
    out = nc.dram_tensor("out_0", (1, S, D), F32, kind="ExternalOutput").ap()
    build(nc, aps, out)
    r = _run(nc, [arrays], core_ids=[0])
    return r.results[0]["out_0"]
```

```python
from contextlib import ExitStack

import concourse.bass as bass
from concourse import mybir

F32 = mybir.dt.float32
F32R = mybir.dt.float32r
I32 = mybir.dt.int32
BF16 = mybir.dt.bfloat16
ALU = mybir.AluOpType
ACT = mybir.ActivationFunctionType
AX = mybir.AxisListType

P = 128
D = 1024
S = 2048
G = 64
C = 16
N = 64
TAU = 8
PR = G // 2
DC = D // P
NT = S // P
GR = 4
EG = 8
NE = GR * EG
FF = D // 2
FC = FF // P
SLOTS = 2 * S + NE * P
NB = SLOTS // P
NBT = NB + 2
EPS = 1e-6
BIG = 1.0e30

BK = 512


def tile_rows(ap, K, tau):
    return ap.rearrange("(k p t) d -> k t p d", k=2, t=TAU)[K, tau]


def same_rows(q):
    g = 8 * (q // 2) + q % 2
    return slice(g, g + 7, 2)


def build_mixer(nc, x, ln_mix, ln_ffn, w_in, lam_re, lam_im, log_dt, b_re, b_im, c_re, c_im,
                d_skip, w_out, w_group, w_expert, h_d, hn_d, W_d, T_d, G_d, ident, rows, gates, blk, region, weights):
    ctx = ExitStack()
    with ctx:
        def sb(name, shape, dt=F32):
            return ctx.enter_context(nc.sbuf_tensor(name, shape, dt))

        def sem(name):
            return ctx.enter_context(nc.semaphore(name))

        R1 = region("R1")
        R2 = region("R2")
        R3 = region("R3")
        R4 = region("R4")
        R5 = region("R5")
        R6 = region("R6")
        R7 = region("R7")
        A4 = sb("A4", [P, 2, 2, PR])
        M4 = sb("M4", [P, 2, 2, PR])
        stats = sb("stats", [P, 64])
        mhalf = sb("mhalf", [P, 2])
        junk = R6[:, 2048:3072]

        w_in_sb = R1[:, :].rearrange("p (k n) -> p k n", k=DC)
        U = [R3[:, :], R4[:, :]]
        St = R5[:, 0:8256].rearrange("p (r q k) -> p r q k", r=2, q=PR)
        LG = R5[:, 8256:8832].rearrange("p (i e) -> p i e", i=NT)
        wr = R5[:, 8832:9120].rearrange("p (k e) -> p k e", k=DC)
        T2 = R5[:, 9120:9184].rearrange("p (r q) -> p r q", r=2)
        xt = [R7[:, 1024 * j:1024 * (j + 1)] for j in range(2)]
        xn = [R7[:, 2048 + 1024 * j:3072 + 1024 * j] for j in range(2)]
        hT = [R7[:, 4096 + 1024 * j:5120 + 1024 * j] for j in range(2)]
        wb = [R6[:, 1024 * j:1024 * (j + 1)] for j in range(2)]
        tgb = [R6[:, 2048 * j:2048 * (j + 1)] for j in range(2)]
        sg = R6[:, 0:1024]
        hn2 = R6[:, 1024:2048]
        hn2T = R6[:, 2048:3072]
        gB = R6[:, 3072:4096]
        ssq = stats[:, 0:16]
        rstd = stats[:, 16:32]
        ssq2 = stats[:, 32:48]
        rstd2 = stats[:, 48:64]

        TP = ctx.enter_context(nc.psum_tensor("TP", [P, D], F32))
        UP = [ctx.enter_context(nc.psum_tensor(f"UP{j}", [P, D], F32)) for j in range(2)]
        AX2 = [ctx.enter_context(nc.psum_tensor(f"AX{j}", [P, BK], F32)) for j in range(2)]

        E = R3[:, 0:576].rearrange("p (r q j) -> p r q j", r=2, q=PR)
        Er = R3[:, 576:1088].rearrange("p (r q j) -> p r q j", r=2, q=PR)
        cf = R3[:, 1088:1216].rearrange("p (v q) -> p v q", v=4)
        Bb = R3[:, 1216:2240].rearrange("p (r q c) -> p r q c", r=2, q=PR)
        Cs = R3[:, 2240:3264].rearrange("p (r q c) -> p r q c", r=2, q=PR)
        Braw = R3[:, 3264:4288].rearrange("p (r q c) -> p r q c", r=2, q=PR)
        tw = R3[:, 4288:5440]
        tz = R3[:, 5440:6592]
        Dc = R3[0:C, 6592:6656]
        dstep = R3[0:C, 6656:7680].rearrange("p (g c) -> p g c", g=G)
        zero = R3[:, 6656:7680]
        L = R2[0:PR, 0:128]
        pv = R2[0:PR, 0:4096].rearrange("p (v n) -> p v n", v=32)
        Cn = R2[:, 4096:5120].rearrange("p (r t n) -> p r t n", r=2, t=4)
        Wst = R4[:, :].rearrange("p (r q t c) -> p r q t c", r=2, q=PR, t=TAU)
        KR = R4[0:C, :].rearrange("p (g m) -> p g m", g=G)
        Gst = R5[:, :].rearrange("p (r q j c) -> p r q j c", r=2, q=PR, j=TAU + 1)

        at = [0]

        def rv(*shape):
            n = 1
            for d in shape:
                n *= d
            v = R2[:, at[0]:at[0] + n]
            at[0] += n
            names = "abcd"[:len(shape)]
            return v.rearrange("p (" + " ".join(names) + ") -> p " + " ".join(names),
                               **{c: d for c, d in zip(names, shape)}) if len(shape) > 1 else v

        rt_og, rt_d = rv(NT, GR), rv(NT, GR)
        rt_o1, rt_o2, rt_c, rt_ein = rv(NT, EG), rv(NT, EG), rv(NT, EG), rv(NT, EG)
        rt_gm, rt_mn, rt_m1, rt_m2, rt_x = rv(NT), rv(NT), rv(NT), rv(NT), rv(NT)
        rt_e4 = rv(NT, EG, GR)
        rt_M1, rt_M2, rt_M, rt_P, rt_S = rv(NT, NE), rv(NT, NE), rv(NT, NE), rv(NT, NE), rv(NT, NE)
        rt_tot, rt_nb, rt_one, rt_be, rt_bs = rv(NE), rv(NE), rv(NE), rv(NE), rv(NE)
        rt_ci = rv(NE).bitcast(I32)
        rt_sf = rv(NT, 2)
        slots = rv(NT, 2).bitcast(I32)
        rt_lo, rt_hi = rv(NT, 2).bitcast(I32), rv(NT, 2).bitcast(I32)
        rt_bk = rv(NE)
        rt_eb = rv(3)
        rt_b1 = rv(1)
        assert at[0] <= 8192 and NBT < P
        tri, ones = R4[:, 0:P], R4[:, P:2 * P]
        ioi = R4[:, 256:256 + P].bitcast(I32)
        iof = R4[:, 384:384 + P]
        tid = R4[:, 512:512 + 2 * NT].bitcast(I32)
        zi = R4[:, 600:600 + NBT].bitcast(I32)
        pi = R4[:, 680:681].bitcast(I32)
        pf = R4[:, 690:691]
        tidf = R4[:, 700:700 + 2 * NT].rearrange("p (i j) -> p i j", j=2)
        zf = R4[:, 800:800 + NBT]
        lof = R4[:, 900:900 + 2 * NT].rearrange("p (i j) -> p i j", j=2)
        hif = R4[:, 950:950 + 2 * NT].rearrange("p (i j) -> p i j", j=2)
        free = R4[:, 1000:1000 + NBT]
        ohP = R5[:, 0:2 * NT * P].rearrange("p (i j m) -> p i j m", i=NT, j=2)
        ohB = R5[:, 2 * NT * P:2 * NT * (P + NBT)].rearrange("p (i j b) -> p i j b", i=NT, j=2)

        s_par = sem("params_loaded")
        s_bc = sem("b_and_d_loaded")
        s_c = sem("c_loaded")
        s_win = sem("w_in_loaded")
        s_gm = sem("gain_loaded")
        s_wing = sem("w_in_scaled")
        s_ident = sem("ident_ready")
        s_zero = sem("zero_ready")
        s_x = [sem(f"x_loaded{j}") for j in range(2)]
        s_sq = sem("squares_summed")
        s_rs = sem("rstd_ready")
        s_xn = sem("xn_ready")
        s_tp = sem("x_transposed")
        s_hT = sem("hT_ready")
        s_mm = sem("u_product")
        s_ue = sem("u_stored")
        s_act = sem("setup_act")
        s_dve = sem("dve_chain")
        s_pow = sem("powers_ready")
        s_pt = sem("params_transposed")
        s_ct = sem("c_transposed")
        s_cc = sem("c_copied")
        s_Wr = sem("W_products")
        s_Gr = sem("G_products")
        s_wt = sem("W_transposed")
        s_wc = sem("W_copied")
        s_wd = [sem(f"W_stored{j}") for j in range(2)]
        s_tz = sem("T_zeroed")
        s_kr = sem("KR_product")
        s_kc = sem("KR_copied")
        s_krd = sem("KR_with_skip")
        s_td = sem("T_stored")
        s_gd = sem("G_stored")
        s_ut = sem("u_transposed")
        s_uv = sem("U_copied_dve")
        s_ua = sem("U_copied_act")
        s_wl = [sem(f"W_loaded{j}") for j in range(2)]
        s_v = sem("states_collected")
        s_vr = sem("states_re_copied")
        s_vi = sem("states_im_copied")
        s_s0 = sem("carry_ready")
        s_sc = sem("scan_steps")
        s_scd = sem("scan_done")
        s_tg = [sem(f"TG_loaded{j}") for j in range(2)]
        s_y = sem("y_product")
        s_z = sem("z_ready")
        s_wo = sem("w_out_loaded")
        s_zt = sem("z_transposed")
        s_zc = sem("zT_ready")
        s_vg = sem("vg_product")
        s_th = sem("tanh_ready")
        s_hh = sem("h_ready")
        s_g1 = sem("gate_half")
        s_x2 = [sem(f"x2_loaded{j}") for j in range(2)]
        s_sq2 = sem("h_squares")
        s_rs2 = sem("h_rstd")
        s_hn = sem("hn_ready")
        s_hd = [sem(f"h_stored{j}") for j in range(2)]
        s_hnd = sem("hn_stored")
        s_ht = sem("hn_transposed")
        s_hc = sem("hnT_ready")
        s_lg = sem("logits_product")
        s_lc = sem("logits_copied")
        s_gf = sem("ffn_gain_loaded")
        s_wrl = sem("router_weights_loaded")
        s_rt = sem("routing_steps")
        s_re = sem("routing_exponentials")
        s_rk = sem("ranks_ready")
        s_tri = sem("routing_constants")
        s_tb = sem("tables")
        s_oh = sem("one_hot_rows")

        xdma = lambda i: tile_rows(x, i // TAU, i % TAU)
        W_v = W_d.rearrange("(b p) n -> b p n", p=P)
        T_v = T_d.rearrange("p (b n) -> b p n", b=8)
        G_v = G_d.rearrange("(r p) (b n) -> b r p n", r=2, b=8)

        block = ctx.enter_context(nc.Block())

        @block.sync
        def _(sp):
            sp.dma_start(pv[:, 0, :], lam_re.rearrange("(q a) n -> q (a n)", a=2)).then_inc(s_par, 16)
            sp.dma_start(pv[:, 1, :], lam_im.rearrange("(q a) n -> q (a n)", a=2)).then_inc(s_par, 16)
            sp.dma_start(pv[:, 2, 0:2], log_dt.rearrange("(q a) -> q a", a=2)).then_inc(s_par, 16)
            sp.dma_start(xt[0], xdma(0)).then_inc(s_x[0], 16)
            sp.dma_start(w_in_sb, w_in.rearrange("(k p) n -> p k n", p=P)).then_inc(s_win, 16)
            sp.dma_start(xt[1], xdma(1)).then_inc(s_x[1], 16)
            sp.wait_ge(s_zero, 1)
            for b in range(8):
                sp.dma_start(T_v[b], zero).then_inc(s_tz, 16)

            def load_x(i):
                sp.wait_ge(s_xn, i - 1)
                sp.dma_start(xt[i % 2], xdma(i)).then_inc(s_x[i % 2], 16)

            for i in range(2, TAU + 2):
                load_x(i)
            for b in range(8):
                sp.wait_ge(s_wc, 4 * b + 4)
                sp.dma_start(W_v[b], wb[b % 2]).then_inc(s_wd[b % 2], 16)
            sp.wait_ge(s_Gr, 2)
            for r in range(2):
                sp.dma_start(G_d.rearrange("(r p) (q x) -> r p q x", r=2, x=P)[r],
                             Gst[:, r, :, 1:9, :].rearrange("p q j c -> p q (j c)")).then_inc(s_gd, 16)
            sp.wait_ge(s_krd, 1)
            sp.wait_ge(s_tz, 16 * 8)
            for t in range(TAU):
                sp.dma_start(T_d.rearrange("(t c) (g m) -> t c g m", t=TAU, g=G)[t][:, :, C * t:P],
                             KR[:, :, 0:P - C * t]).then_inc(s_td, 16)

            def load_w(K):
                for b in range(8):
                    if b >= 2 or K == 1:
                        sp.wait_ge(s_v, 16 * K + 2 * (b - 2) + 2)
                    elif K == 0:
                        sp.wait_ge(s_wd[0], 64)
                        sp.wait_ge(s_wd[1], 64)
                    sp.dma_start(wb[b % 2], W_v[b]).then_inc(s_wl[b % 2], 16)

            def load_tg(K):
                for b in range(8):
                    if b >= 2:
                        sp.wait_ge(s_y, 16 * K + 2 * (b - 2) + 2)
                    t = tgb[b % 2]
                    sp.dma_start(t[:, 0:1024], T_v[b]).then_inc(s_tg[b % 2], 16)
                    sp.dma_start(t[:, 1024:1536], G_v[b, 0]).then_inc(s_tg[b % 2], 16)
                    sp.dma_start(t[:, 1536:2048], G_v[b, 1]).then_inc(s_tg[b % 2], 16)

            load_w(0)
            for i in range(TAU + 2, NT):
                load_x(i)
            sp.wait_ge(s_mm, NT)
            wo_v = w_out.rearrange("(k p) n -> p k n", p=P)
            sp.dma_start(R1[:, :].rearrange("p (k n) -> p k n", k=4), wo_v[:, 0:4, :]).then_inc(s_wo, 16)
            sp.wait_ge(s_gd, 32)
            sp.wait_ge(s_td, 16 * 8)
            sp.wait_ge(s_v, 16)
            load_tg(0)
            sp.wait_ge(s_y, 16)
            load_w(1)
            sp.dma_start(R3[:, :].rearrange("p (k n) -> p k n", k=4), wo_v[:, 4:8, :]).then_inc(s_wo, 16)

            def load_x2(i):
                if i >= 2:
                    sp.wait_ge(s_hh, 2 * (i - 2) + 2)
                else:
                    sp.wait_ge(s_xn, NT)
                sp.dma_start(xt[i % 2], xdma(i)).then_inc(s_x2[i % 2], 16)

            def gate_tiles(K):
                for i in range(TAU * K, TAU * K + TAU):
                    if K == 0 and i == 0:
                        load_x2(0)
                        load_x2(1)
                        sp.wait_ge(s_v, 32)
                    if i == TAU * K:
                        sp.dma_start(gB, ln_ffn.partition_broadcast(P)).then_inc(s_gf, 16)
                    sp.wait_ge(s_hh, 2 * i + 2)
                    sp.dma_start(tile_rows(h_d, i // TAU, i % TAU), xn[i % 2]).then_inc(s_hd[i % 2], 16)
                    if i + 2 < NT:
                        load_x2(i + 2)
                    sp.wait_ge(s_hn, i + 1)
                    sp.dma_start(tile_rows(hn_d, i // TAU, i % TAU), hn2).then_inc(s_hnd, 16)

            gate_tiles(0)
            sp.wait_ge(s_hnd, 16 * TAU)
            sp.wait_ge(s_hc, TAU)
            sp.wait_ge(s_lg, TAU)
            load_tg(1)
            sp.wait_ge(s_y, 32)
            gate_tiles(1)
            sp.wait_ge(s_hnd, 16 * NT)
            for j in range(2):
                sp.wait_ge(s_hd[j], 16 * NT // 2)
            sp.wait_ge(s_sq2, NT)
            sp.wait_ge(s_vg, 2 * NT)
            for j in range(NPC):
                if j >= RAW:
                    sp.wait_ge(region.s_pL, j + 1 - RAW)
                region.load_piece(sp, weights, 0, j)

        @block.gpsimd
        def _(pool):
            nc.gpsimd.memset(ident[:, :], 0.0).then_inc(s_ident, 1)
            nc.gpsimd.memset(mhalf[:, :], -0.5).then_inc(s_ident, 1)
            nc.gpsimd.memset(zero, 0.0).then_inc(s_zero, 1)
            pool.wait_ge(s_ident, 2)
            nc.gpsimd.affine_select(out=ident[:, :], in_=ident[:, :], compare_op=ALU.not_equal, fill=1.0,
                                    base=0, pattern=[[-1, P]], channel_multiplier=1).then_inc(s_ident, 1)
            pool.wait_ge(s_ident, 3)
            with nc.allow_non_contiguous_dma(reason="a few thousand parameters"):
                gmixT = M4[:, 0, 0, 0:DC]
                pool.dma_start(gmixT, ln_mix.rearrange("(k p) -> p k", p=P)).then_inc(s_gm, 16)
                for a in range(2):
                    for r, src in enumerate((b_re, b_im)):
                        pool.dma_start(Braw[N * a:N * a + N, r], src.rearrange("(q a) n c -> a n q c", a=2)[a]).then_inc(s_bc, 16)
                pool.dma_start(Dc, d_skip.rearrange("(g c) -> c g", c=C)).then_inc(s_bc, 16)

            def stat(i, src, dst, s_from, s_to):
                pool.wait_ge(s_from, i + 1)
                nc.gpsimd.tensor_scalar(dst[:, i:i + 1], src[:, i:i + 1], 1.0 / D, EPS, ALU.mult, ALU.add).then_inc(s_to, 1)
                pool.wait_ge(s_to, 2 * i + 1)
                nc.gpsimd.tensor_tensor(out=dst[:, i:i + 1], in0=dst[:, i:i + 1], in1=mhalf[:, 0:1], op=ALU.pow).then_inc(s_to, 1)

            for i in range(NT):
                stat(i, ssq, rstd, s_sq, s_rs)
            with nc.allow_non_contiguous_dma(reason="router weights"):
                pool.wait_ge(s_gd, 32)
                pool.dma_start(wr[:, :, 0:GR], w_group.rearrange("(k p) e -> p k e", p=P)).then_inc(s_wrl, 16)
                pool.dma_start(wr[:, :, GR:GR + NE], w_expert.rearrange("(k p) e -> p k e", p=P)).then_inc(s_wrl, 16)
            for i in range(NT):
                if i == TAU:
                    pool.wait_ge(s_y, 32)
                    nc.gpsimd.memset(ones, 1.0).then_inc(s_tri, 1)
                    pool.wait_ge(s_tri, 1)
                    nc.gpsimd.affine_select(out=tri, in_=ones, compare_op=ALU.is_gt, fill=0.0, base=0,
                                            pattern=[[1, P]], channel_multiplier=-1).then_inc(s_tri, 1)
                    nc.gpsimd.iota(ioi, pattern=[[1, P]], base=0, channel_multiplier=0).then_inc(s_tri, 1)
                    nc.gpsimd.iota(tid, pattern=[[S // 2, 2], [1, TAU], [S, 2]], base=1, channel_multiplier=TAU).then_inc(s_tri, 1)
                    nc.gpsimd.iota(pi, pattern=[[1, 1]], base=0, channel_multiplier=1).then_inc(s_tri, 1)
                    nc.gpsimd.iota(zi, pattern=[[P, NBT]], base=2 * S + 1, channel_multiplier=1).then_inc(s_tri, 1)
                stat(i, ssq2, rstd2, s_sq2, s_rs2)
            for j in range(EARLY):
                pool.wait_ge(region.s_pH, j + 1)
                at = slice(2 * PC * j, 2 * PC * j + PC)
                nc.gpsimd.tensor_tensor(out=region.wL[:, at], in0=region.raw[j % RAW], in1=region.wH[:, at].bitcast(F32),
                                        op=ALU.subtract).then_inc(region.s_pL, 1)

        @block.scalar
        def _(act):
            for r, src in enumerate((c_re, c_im)):
                v = src.rearrange("(t q a) c n -> t a q c n", t=4, a=2)
                for t in range(4):
                    for a in range(2):
                        act.dma_start(Cn[:, r, t, N * a:N * a + N], v[t, a]).then_inc(s_c, 16)
            act.wait_ge(s_par, 48)
            nc.scalar.activation(pv[:, 3, 0:2], pv[:, 2, 0:2], ACT.Exp).then_inc(s_act, 1)
            act.wait_ge(s_dve, 3)
            nc.scalar.activation(pv[:, 7, :], pv[:, 5, :], ACT.Exp).then_inc(s_act, 1)
            act.wait_ge(s_dve, 13)
            nc.scalar.activation(pv[:, 12, :], pv[:, 9, :], ACT.Sin).then_inc(s_act, 1)
            nc.scalar.activation(pv[:, 13, :], pv[:, 10, :], ACT.Sin).then_inc(s_act, 1)

            def square(i):
                act.wait_ge(s_x[i % 2], 16 * (i // 2 + 1))
                if i > 0:
                    act.wait_ge(s_sq, i)
                nc.scalar.activation(junk, xt[i % 2], ACT.Square, accum_out=ssq[:, i:i + 1]).then_inc(s_sq, 1)

            def normalise(i):
                act.wait_ge(s_rs, 2 * i + 2)
                if i >= 2:
                    act.wait_ge(s_tp, i - 1)
                nc.scalar.activation(xn[i % 2], xt[i % 2], ACT.Copy, scale=rstd[:, i:i + 1]).then_inc(s_xn, 1)

            def copy_hT(i):
                act.wait_ge(s_tp, i + 1)
                if i >= 2:
                    act.wait_ge(s_mm, i - 1)
                nc.scalar.activation(hT[i % 2], TP[:, :], ACT.Copy).then_inc(s_hT, 1)

            def store_u(i):
                act.wait_ge(s_mm, i + 1)
                if i == TAU:
                    act.wait_ge(s_ut, 16)
                if i == 0:
                    act.wait_ge(s_ct, 2)
                    act.wait_ge(s_pt, 1)
                nc.scalar.activation(R2[:, :].rearrange("p (g t c) -> p t g c", g=G, t=TAU)[:, i % TAU],
                                     UP[i % 2][:, :].rearrange("p (g c) -> p g c", g=G), ACT.Copy).then_inc(s_ue, 1)

            def copy_U(K):
                for q in range(1, 16, 2):
                    act.wait_ge(s_ut, 16 * K + q + 1)
                    nc.scalar.activation(U[K][:, BK * q:BK * q + BK], AX2[q % 2][:, :], ACT.Copy).then_inc(s_ua, 1)

            def copy_states_im(K):
                for q in range(16):
                    act.wait_ge(s_v, 16 * K + q + 1)
                    if q == 0:
                        act.wait_ge(s_s0, K + 1)
                    ps = AX2[q % 2][N:P, :].rearrange("n (q a k) -> n q a k", q=2, a=2)
                    for a in range(2):
                        last = nc.scalar.activation(St[N * a:N * a + N, 1, 2 * q:2 * q + 2, 1:129], ps[:, :, a, :], ACT.Copy)
                    last.then_inc(s_vi, 1)

            def phase1(K):
                for i in range(TAU * K, TAU * K + TAU):
                    if i + 1 < NT:
                        copy_hT(i + 1)
                    if i + 2 < NT:
                        square(i + 2)
                        normalise(i + 2)
                    store_u(i)

            square(0)
            normalise(0)
            copy_hT(0)
            square(1)
            normalise(1)
            phase1(0)
            for q in range(16):
                act.wait_ge(s_wt, q + 1)
                b = q // 2
                if b >= 2 and q % 2 == 0:
                    act.wait_ge(s_wd[b % 2], 16 * (b // 2))
                for l in range(2):
                    dst = wb[b % 2].rearrange("p (q a r n) -> p q r a n", q=4, a=2, r=2)[:, 2 * (q % 2) + l]
                    nc.scalar.activation(dst, AX2[q % 2][:, 256 * l:256 * l + 256].rearrange("p (r a n) -> p r a n", r=2, a=2),
                                         ACT.Copy).then_inc(s_wc, 1)
            copy_U(0)
            copy_states_im(0)
            phase1(1)
            copy_U(1)

            def gelu(K):
                for q in range(16):
                    act.wait_ge(s_y, 16 * K + q + 1)
                    z = R2[:, :].rearrange("p (t g c) -> p g t c", t=TAU, g=G)[:, same_rows(q)]
                    if q == 0:
                        act.wait_ge(s_ut, 32)
                        if K == 1:
                            act.wait_ge(s_zt, TAU)
                    nc.scalar.activation(z, AX2[q % 2][:, :].rearrange("p (g t c) -> p g t c", g=4, t=TAU),
                                         ACT.Gelu_apprx_tanh).then_inc(s_z, 1)

            def tanh_half(i, nh):
                act.wait_ge(s_vg, 2 * i + nh + 1)
                if i >= 1:
                    act.wait_ge(s_hh, 2 * (i - 1) + nh + 1)
                nc.scalar.activation(sg[:, BK * nh:BK * nh + BK], UP[nh][:, BK:2 * BK], ACT.Tanh, scale=0.5).then_inc(s_th, 1)

            def square_h(i):
                act.wait_ge(s_hh, 2 * i + 2)
                nc.scalar.activation(R2[:, D * (i % TAU):D * (i % TAU) + D], xn[i % 2], ACT.Square,
                                     accum_out=ssq2[:, i:i + 1]).then_inc(s_sq2, 1)

            def copy_zT(i):
                act.wait_ge(s_zt, i + 1)
                nc.scalar.activation(hT[i % 2], TP[:, :], ACT.Copy).then_inc(s_zc, 1)

            def copy_hnT(i):
                act.wait_ge(s_ht, i + 1)
                if i >= 1:
                    act.wait_ge(s_lg, i)
                nc.scalar.activation(hn2T, TP[:, :], ACT.Copy).then_inc(s_hc, 1)

            def copy_logits(i):
                act.wait_ge(s_lg, i + 1)
                nc.scalar.activation(LG[:, i, :], AX2[0][:, 0:GR + NE], ACT.Copy).then_inc(s_lc, 1)

            for K in range(2):
                gelu(K)
                if K == 0:
                    copy_states_im(1)
                t0 = TAU * K
                copy_zT(t0)
                for i in range(t0, t0 + TAU):
                    if i > t0:
                        copy_hnT(i - 1)
                    tanh_half(i, 0)
                    if i > t0:
                        copy_logits(i - 1)
                    if i + 1 < t0 + TAU:
                        copy_zT(i + 1)
                    tanh_half(i, 1)
                    square_h(i)
                copy_hnT(t0 + TAU - 1)
                copy_logits(t0 + TAU - 1)
            act.wait_ge(s_rt, 1)
            nc.scalar.activation(rt_d, rt_d, ACT.Exp).then_inc(s_re, 1)
            act.wait_ge(s_rt, 2)
            nc.scalar.activation(rt_x, rt_x, ACT.Exp).then_inc(s_re, 1)
            for j in range(EARLY):
                act.wait_ge(region.s_raw[j % RAW], 32 * (j // RAW + 1))
                nc.scalar.activation(region.wH[:, 2 * PC * j:2 * PC * j + PC], region.raw[j % RAW],
                                     ACT.Copy).then_inc(region.s_pH, 1)

        @block.vector
        def _(dve):
            chain = [0]

            def link(ins):
                chain[0] += 1
                ins.then_inc(s_dve, 1)
                dve.wait_ge(s_dve, chain[0])

            def dt_of(ap):
                return ap[:, :].unsqueeze(2).broadcast_to([PR, 2, N])

            v2 = lambda j: pv[:, j, :].rearrange("q (a n) -> q a n", a=2)
            ts, tt = nc.vector.tensor_scalar, nc.vector.tensor_tensor
            dve.wait_ge(s_par, 48)
            link(ts(pv[:, 4, :], pv[:, 0, :], -1e-4, None, ALU.min))
            dve.wait_ge(s_act, 1)
            link(tt(out=v2(5), in0=v2(4), in1=dt_of(pv[:, 3, 0:2]), op=ALU.mult))
            link(tt(out=v2(6), in0=v2(1), in1=dt_of(pv[:, 3, 0:2]), op=ALU.mult))
            MAGIC = 12582912.0
            link(ts(pv[:, 8, :], pv[:, 6, :], 0.15915494309189535, MAGIC, ALU.mult, ALU.add))
            link(ts(pv[:, 8, :], pv[:, 8, :], -MAGIC, None, ALU.add))
            link(ts(pv[:, 9, :], pv[:, 8, :], -6.28125, None, ALU.mult))
            link(tt(out=pv[:, 9, :], in0=pv[:, 9, :], in1=pv[:, 6, :], op=ALU.add))
            for part in (0.0019350051879882812, 3.019916050561733e-07):
                link(nc.vector.scalar_tensor_tensor(out=pv[:, 9, :], in0=pv[:, 8, :], scalar=-part, in1=pv[:, 9, :],
                                                    op0=ALU.mult, op1=ALU.add))
            link(ts(pv[:, 9, :], pv[:, 9, :], 3.1415925, -3.1415925, ALU.min, ALU.max))
            link(ts(pv[:, 10, :], pv[:, 9, :], -1.0, None, ALU.mult))
            link(tt(out=pv[:, 10, :], in0=pv[:, 10, :], in1=pv[:, 9, :], op=ALU.max))
            link(ts(pv[:, 10, :], pv[:, 10, :], -1.0, 1.5707963267948966, ALU.mult, ALU.add))
            assert chain[0] == 13
            link(tt(out=pv[:, 14, :], in0=pv[:, 4, :], in1=pv[:, 4, :], op=ALU.mult))
            link(tt(out=pv[:, 15, :], in0=pv[:, 1, :], in1=pv[:, 1, :], op=ALU.mult))
            link(tt(out=pv[:, 14, :], in0=pv[:, 14, :], in1=pv[:, 15, :], op=ALU.add))
            link(nc.vector.reciprocal(pv[:, 14, :], pv[:, 14, :]))
            dve.wait_ge(s_act, 4)
            link(tt(out=pv[:, 16, :], in0=pv[:, 7, :], in1=pv[:, 13, :], op=ALU.mult))
            link(tt(out=pv[:, 17, :], in0=pv[:, 7, :], in1=pv[:, 12, :], op=ALU.mult))
            link(ts(pv[:, 20, :], pv[:, 16, :], -1.0, None, ALU.add))
            link(tt(out=pv[:, 21, :], in0=pv[:, 20, :], in1=pv[:, 4, :], op=ALU.mult))
            link(tt(out=pv[:, 22, :], in0=pv[:, 17, :], in1=pv[:, 1, :], op=ALU.mult))
            link(tt(out=pv[:, 21, :], in0=pv[:, 21, :], in1=pv[:, 22, :], op=ALU.add))
            link(tt(out=pv[:, 18, :], in0=pv[:, 21, :], in1=pv[:, 14, :], op=ALU.mult))
            link(tt(out=pv[:, 21, :], in0=pv[:, 17, :], in1=pv[:, 4, :], op=ALU.mult))
            link(tt(out=pv[:, 22, :], in0=pv[:, 20, :], in1=pv[:, 1, :], op=ALU.mult))
            link(tt(out=pv[:, 21, :], in0=pv[:, 21, :], in1=pv[:, 22, :], op=ALU.subtract))
            link(tt(out=pv[:, 19, :], in0=pv[:, 21, :], in1=pv[:, 14, :], op=ALU.mult))
            dve.sem_inc(s_pow, 1)
            dve.wait_ge(s_win, 16)
            dve.wait_ge(s_gm, 16)
            for k in range(DC):
                ts(w_in_sb[:, k, :], w_in_sb[:, k, :], M4[:, 0, 0, k:k + 1], None, ALU.mult).then_inc(s_wing, 1)
            dve.wait_ge(s_pt, 1)
            link(nc.vector.tensor_copy(cf, AX2[0][:, 0:128].rearrange("p (v q) -> p v q", v=4)))
            for r in range(2):
                dve.wait_ge(s_ct, r + 1)
                src = (AX2[1] if r == 0 else UP[1])[:, 0:BK]
                link(nc.vector.tensor_copy(Cs[:, r], src.rearrange("p (q c) -> p q c", q=PR)))
                dve.sem_inc(s_cc, 1)
            link(nc.vector.memset(E[:, 0, :, 0], 1.0))
            link(nc.vector.memset(E[:, 1, :, 0], 0.0))
            link(nc.vector.tensor_copy(E[:, :, :, 1], cf[:, 0:2, :]))

            def cmul(re, im, ar, ai, br, bi, t0, t1, neg_im=False):
                link(tt(out=t0, in0=ar, in1=br, op=ALU.mult))
                link(tt(out=t1, in0=ai, in1=bi, op=ALU.mult))
                link(tt(out=re, in0=t0, in1=t1, op=ALU.subtract))
                link(tt(out=t0, in0=ar, in1=bi, op=ALU.mult))
                link(tt(out=t1, in0=ai, in1=br, op=ALU.mult))
                if neg_im:
                    link(nc.vector.scalar_tensor_tensor(out=im, in0=t0, scalar=-1.0, in1=t1, op0=ALU.mult, op1=ALU.subtract))
                else:
                    link(tt(out=im, in0=t0, in1=t1, op=ALU.add))

            for j in range(2, TAU + 1):
                cmul(E[:, 0, :, j], E[:, 1, :, j], E[:, 0, :, j - 1], E[:, 1, :, j - 1], cf[:, 0, :], cf[:, 1, :],
                     tw[:, 0:PR], tz[:, 0:PR])
            for t in range(TAU):
                link(nc.vector.tensor_copy(Er[:, :, :, t], E[:, :, :, TAU - 1 - t]))
            link(nc.vector.tensor_copy(A4[:, 0, 0, :], E[:, 0, :, TAU]))
            link(nc.vector.tensor_copy(A4[:, 1, 1, :], E[:, 0, :, TAU]))
            link(nc.vector.tensor_copy(A4[:, 1, 0, :], E[:, 1, :, TAU]))
            link(ts(A4[:, 0, 1, :], E[:, 1, :, TAU], -1.0, None, ALU.mult))
            dve.wait_ge(s_bc, 16 * 5)
            gb = lambda r: cf[:, 2 + r, :].unsqueeze(2).broadcast_to([P, PR, C])
            v16 = lambda t: t[:, 0:PR * C].rearrange("p (q c) -> p q c", q=PR)
            cmul(Bb[:, 0], Bb[:, 1], gb(0), gb(1), Braw[:, 0], Braw[:, 1], v16(tw), v16(tz))
            for q in range(0, PR, 8):
                e = lambda r: Er[:, r, q:q + 8, :].unsqueeze(3).broadcast_to([P, 8, TAU, C])
                bb = lambda r: Bb[:, r, q:q + 8, :].unsqueeze(2).broadcast_to([P, 8, TAU, C])
                v = lambda t: t[:, 0:1024].rearrange("p (q t c) -> p q t c", q=8, t=TAU)
                cmul(Wst[:, 0, q:q + 8], Wst[:, 1, q:q + 8], e(0), e(1), bb(0), bb(1), v(tw), v(tz))
                dve.sem_inc(s_Wr, 1)
            for q in range(0, PR, 8):
                e = lambda r: E[:, r, q:q + 8, :].unsqueeze(3).broadcast_to([P, 8, TAU + 1, C])
                cc = lambda r: Cs[:, r, q:q + 8, :].unsqueeze(2).broadcast_to([P, 8, TAU + 1, C])
                v = lambda t: t[:, 0:1152].rearrange("p (q t c) -> p q t c", q=8, t=TAU + 1)
                cmul(Gst[:, 0, q:q + 8], Gst[:, 1, q:q + 8], e(0), e(1), cc(0), cc(1), v(tw), v(tz), neg_im=True)
            dve.sem_inc(s_Gr, 2)
            dve.wait_ge(s_tz, 16 * 8)
            link(tt(out=dstep, in0=ident[0:C, 0:C].unsqueeze(1).broadcast_to([C, G, C]),
                    in1=Dc.unsqueeze(2).broadcast_to([C, G, C]), op=ALU.mult))
            for q in range(16):
                dve.wait_ge(s_kr, q + 1)
                nc.vector.tensor_copy(KR[:, same_rows(q), :],
                                      AX2[q % 2][0:C, :].rearrange("c (g m) -> c g m", g=4)).then_inc(s_kc, 1)
            dve.wait_ge(s_kc, 16)
            tt(out=KR[:, :, 0:C], in0=KR[:, :, 0:C], in1=dstep, op=ALU.add).then_inc(s_krd, 1)

            def copy_U(K):
                for q in range(0, 16, 2):
                    dve.wait_ge(s_ut, 16 * K + q + 1)
                    nc.vector.tensor_copy(U[K][:, BK * q:BK * q + BK], AX2[q % 2][:, :]).then_inc(s_uv, 1)

            def copy_states_re(K):
                if K == 1:
                    dve.wait_ge(s_y, 16)
                    link(nc.vector.tensor_copy(St[:, :, :, 0], St[:, :, :, 128]))
                else:
                    dve.wait_ge(s_gd, 32)
                    dve.wait_ge(s_kr, 16)
                    link(nc.vector.memset(St[:, :, :, 0], 0.0))
                dve.sem_inc(s_s0, 1)
                for q in range(16):
                    dve.wait_ge(s_v, 16 * K + q + 1)
                    ps = AX2[q % 2][0:N, :].rearrange("n (q a k) -> n q a k", q=2, a=2)
                    for a in range(2):
                        last = nc.vector.tensor_copy(St[N * a:N * a + N, 0, 2 * q:2 * q + 2, 1:129], ps[:, :, a, :])
                    last.then_inc(s_vr, 1)

            def scan(K, first, count):
                if first == 0:
                    dve.wait_ge(s_vr, 16 * (K + 1))
                    dve.wait_ge(s_vi, 16 * (K + 1))
                base = 3 * (128 * K + first)
                body = 16 if K == 0 else 8
                with dve.Fori(0, count // body) as j:
                    for c in range(body):
                        k = body * j + (first + c)
                        n = 3 * body * j + (base + 3 * c)
                        old = St[:, :, :, bass.ds(k, 1)].rearrange("p r q o -> p r (q o)")
                        new = St[:, :, :, bass.ds(k + 1, 1)].rearrange("p r q o -> p r (q o)")
                        tt(out=M4[:, :, :, :], in0=A4[:, :, :, :], in1=old.unsqueeze(1).broadcast_to([P, 2, 2, PR]),
                           op=ALU.mult).then_inc(s_sc, 1)
                        dve.wait_ge(s_sc, n + 1)
                        tt(out=T2, in0=M4[:, :, 0, :], in1=M4[:, :, 1, :], op=ALU.add).then_inc(s_sc, 1)
                        dve.wait_ge(s_sc, n + 2)
                        tt(out=new, in0=new, in1=T2, op=ALU.add).then_inc(s_sc, 1)
                        dve.wait_ge(s_sc, n + 3)
                if first + count == 128:
                    dve.sem_inc(s_scd, 1)

            copy_U(0)
            copy_states_re(0)
            scan(0, 0, 128)
            copy_U(1)

            def gate_tile(i):
                h = xn[i % 2]
                for nh in range(2):
                    f = slice(BK * nh, BK * nh + BK)
                    dve.wait_ge(s_th, 2 * i + nh + 1)
                    nc.vector.scalar_tensor_tensor(out=sg[:, f], in0=sg[:, f], scalar=1.0, in1=UP[nh][:, 0:BK],
                                                   op0=ALU.add, op1=ALU.mult).then_inc(s_g1, 1)
                for nh in range(2):
                    f = slice(BK * nh, BK * nh + BK)
                    dve.wait_ge(s_g1, 2 * i + nh + 1)
                    if nh == 0:
                        dve.wait_ge(s_x2[i % 2], 16 * (i // 2 + 1))
                        if i >= 2:
                            dve.wait_ge(s_hd[i % 2], 16 * (i // 2))
                    nc.vector.scalar_tensor_tensor(out=h[:, f], in0=sg[:, f], scalar=0.5, in1=xt[i % 2][:, f],
                                                   op0=ALU.mult, op1=ALU.add).then_inc(s_hh, 1)
                dve.wait_ge(s_rs2, 2 * i + 2)
                dve.wait_ge(s_gf, 16 * (i // TAU + 1))
                if i >= 1:
                    dve.wait_ge(s_hnd, 16 * i)
                    dve.wait_ge(s_ht, i)
                nc.vector.scalar_tensor_tensor(out=hn2, in0=h, scalar=rstd2[:, i:i + 1], in1=gB,
                                               op0=ALU.mult, op1=ALU.mult).then_inc(s_hn, 1)

            copy_states_re(1)
            for i in range(NT):
                if i < TAU:
                    scan(1, 16 * i, 16)
                gate_tile(i)

            red = nc.vector.tensor_reduce
            stt = nc.vector.scalar_tensor_tensor
            dve.wait_ge(s_lc, NT)
            dve.wait_ge(s_tri, 6)
            dve.wait_ge(s_zt, NT)
            dve.wait_ge(s_sq2, NT)
            bc = lambda ap, shape: ap.unsqueeze(len(ap.shape)).broadcast_to(shape)
            link(nc.vector.tensor_copy(iof, ioi))
            link(nc.vector.tensor_copy(tidf.rearrange("p i j -> p (i j)"), tid))
            link(nc.vector.tensor_copy(zf, zi))
            link(nc.vector.tensor_copy(pf, pi))
            link(ts(rt_b1, pf, 1.0, None, ALU.add))
            gl, el = LG[:, :, 0:GR], LG[:, :, GR:GR + NE].rearrange("p i (g j) -> p i g j", g=GR)

            def first_max(oh, v, m, cand, n):
                link(red(m, v, AX.X, ALU.max))
                link(tt(out=oh, in0=v, in1=bc(m, [P, NT, n]), op=ALU.is_ge))
                link(stt(out=cand, in0=oh, scalar=-64.0, in1=iof[:, 0:n].unsqueeze(1).broadcast_to([P, NT, n]),
                         op0=ALU.mult, op1=ALU.add))
                link(red(rt_mn, cand, AX.X, ALU.min))
                link(tt(out=oh, in0=cand, in1=bc(rt_mn, [P, NT, n]), op=ALU.is_equal))

            first_max(rt_og, gl, rt_gm, rt_c[:, :, 0:GR], GR)
            link(tt(out=rt_d, in0=gl, in1=bc(rt_gm, [P, NT, GR]), op=ALU.subtract))
            dve.sem_inc(s_rt, 1)
            link(tt(out=rt_e4, in0=el.rearrange("p i g j -> p i j g"), in1=rt_og.unsqueeze(2).broadcast_to([P, NT, EG, GR]),
                    op=ALU.mult))
            link(red(rt_ein, rt_e4, AX.X, ALU.add))
            first_max(rt_o1, rt_ein, rt_m1, rt_c, EG)
            link(stt(out=rt_ein, in0=rt_o1, scalar=-BIG, in1=rt_ein, op0=ALU.mult, op1=ALU.add))
            first_max(rt_o2, rt_ein, rt_m2, rt_c, EG)
            link(tt(out=rt_x, in0=rt_m2, in1=rt_m1, op=ALU.subtract))
            dve.sem_inc(s_rt, 1)
            dve.wait_ge(s_re, 2)
            link(red(rt_gm, rt_d, AX.X, ALU.add))
            link(nc.vector.reciprocal(rt_gm, rt_gm))
            link(ts(rt_m1, rt_x, 1.0, None, ALU.add))
            link(nc.vector.reciprocal(rt_m1, rt_m1))
            link(tt(out=gates[:, :, 0], in0=rt_gm, in1=rt_m1, op=ALU.mult))
            link(tt(out=gates[:, :, 1], in0=gates[:, :, 0], in1=rt_x, op=ALU.mult))
            for mm, oo in ((rt_M1, rt_o1), (rt_M2, rt_o2)):
                for g in range(GR):
                    link(tt(out=mm[:, :, EG * g:EG * g + EG], in0=oo, in1=rt_og[:, :, g:g + 1].broadcast_to([P, NT, EG]),
                            op=ALU.mult))
            link(tt(out=rt_M, in0=rt_M1, in1=rt_M2, op=ALU.add))
            dve.sem_inc(s_rt, 1)
            link(nc.vector.memset(rt_P[:, 0, :], 0.0))
            for i in range(1, NT):
                link(tt(out=rt_P[:, i, :], in0=rt_P[:, i - 1, :], in1=rt_M[:, i - 1, :], op=ALU.add))
            link(tt(out=rt_tot, in0=rt_P[:, NT - 1, :], in1=rt_M[:, NT - 1, :], op=ALU.add))
            dve.sem_inc(s_rt, 1)
            dve.wait_ge(s_rk, 1)
            link(ts(rt_ci, AX2[1][:, 0:NE], 127.0, None, ALU.add))
            link(ts(rt_ci, rt_ci, 7, None, ALU.arith_shift_right))
            link(ts(rt_nb, rt_ci, 1.0, None, ALU.max))
            link(nc.vector.memset(rt_one, 1.0))
            link(nc.vector.tensor_tensor_scan(rt_be, rt_one, rt_nb, 0.0, ALU.mult, ALU.add))
            link(tt(out=rt_bs, in0=rt_be, in1=rt_nb, op=ALU.subtract))
            link(stt(out=rt_S, in0=rt_bs.unsqueeze(1).broadcast_to([P, NT, NE]), scalar=128.0,
                     in1=AX2[0][:, :].rearrange("p (i e) -> p i e", i=NT), op0=ALU.mult, op1=ALU.add))
            for j, mm in enumerate((rt_M1, rt_M2)):
                link(tt(out=mm, in0=mm, in1=rt_S, op=ALU.mult))
                link(red(rt_sf[:, :, j], mm, AX.X, ALU.add))
            link(nc.vector.tensor_copy(slots, rt_sf))
            link(ts(rt_lo, slots, P - 1, None, ALU.bitwise_and))
            link(ts(rt_hi, slots, 7, None, ALU.arith_shift_right))
            link(nc.vector.tensor_copy(lof, rt_lo))
            link(nc.vector.tensor_copy(hif, rt_hi))
            ramp = lambda n: iof[:, 0:n].unsqueeze(1).broadcast_to([P, 2 * NT, n])
            flat = lambda ap: ap.rearrange("p i j -> p (i j)")
            rows_p, rows_b = (v.rearrange("p i j m -> p (i j) m") for v in (ohP, ohB))
            link(tt(out=rows_b, in0=bc(flat(hif), [P, 2 * NT, NBT]), in1=ramp(NBT), op=ALU.is_equal))
            link(tt(out=rows_b, in0=rows_b, in1=bc(flat(tidf), [P, 2 * NT, NBT]), op=ALU.mult))
            for part in range(4):
                m = slice(part * 2 * NT // 4, (part + 1) * 2 * NT // 4)
                tt(out=rows_p[:, m, :], in0=bc(flat(lof), [P, 2 * NT, P])[:, m, :], in1=ramp(P)[:, m, :],
                   op=ALU.is_equal).then_inc(s_oh, 1)
            be = rt_be
            link(ts(rt_bk, be, pf, None, ALU.is_le))
            link(red(rt_eb[:, 0:1], rt_bk, AX.X, ALU.add))
            link(ts(rt_eb[:, 0:1], rt_eb[:, 0:1], float(NE - 1), None, ALU.min))
            link(ts(rt_bk, be, rt_b1, None, ALU.is_equal))
            link(red(rt_eb[:, 1:2], rt_bk[:, 0:NE - 1], AX.X, ALU.add))
            link(red(rt_eb[:, 2:3], rt_bk[:, 0:NE - 2], AX.X, ALU.add))
            dve.sem_inc(s_rt, 1)
            link(nc.vector.tensor_scalar(blk[:, 3 * NBT:3 * NBT + 1], be[0:1, NE - 1:NE], 1.0, None, ALU.subtract))
            dve.wait_ge(s_tb, 2)
            link(nc.vector.tensor_copy(blk[:, 0:3 * NBT].rearrange("o (v b) -> o v b", v=3),
                                       AX2[0][0:1, 0:3 * P].rearrange("o (v b) -> o v b", v=3)[:, :, 0:NBT]))
            link(stt(out=free, in0=AX2[1][:, 0:NBT], scalar=0.5, in1=zf, op0=ALU.is_lt, op1=ALU.mult))
            link(stt(out=rows, in0=AX2[1][:, 0:NBT], scalar=-1.0, in1=free, op0=ALU.add, op1=ALU.add))

        @block.tensor
        def _(pe):
            pe.wait_ge(s_ident, 3)

            def transpose_x(i):
                pe.wait_ge(s_xn, i + 1)
                if i >= 1:
                    pe.wait_ge(s_hT, i)
                for k in range(DC):
                    last = nc.tensor.transpose(TP[:, P * k:P * k + P], xn[i % 2][:, P * k:P * k + P], ident[:, :])
                last.then_inc(s_tp, 1)

            def product_u(i):
                pe.wait_ge(s_hT, i + 1)
                if i == 0:
                    pe.wait_ge(s_wing, DC)
                if i >= 2:
                    pe.wait_ge(s_ue, i - 1)
                for k in range(DC):
                    for nh in range(2):
                        last = nc.tensor.matmul(UP[i % 2][:, BK * nh:BK * nh + BK], hT[i % 2][:, P * k:P * k + P],
                                                w_in_sb[:, k, BK * nh:BK * nh + BK], start=(k == 0), stop=(k == DC - 1))
                last.then_inc(s_mm, 1)

            def transpose_u(K):
                pe.wait_ge(s_ue, TAU * (K + 1))
                for q in range(16):
                    if q >= 2:
                        if q % 2 == 0:
                            pe.wait_ge(s_uv, 8 * K + q // 2)
                        else:
                            pe.wait_ge(s_ua, 8 * K + q // 2)
                    for g in range(4 * q, 4 * q + 4):
                        last = nc.tensor.transpose(AX2[q % 2][:, P * (g % 4):P * (g % 4) + P],
                                                   R2[:, P * g:P * g + P], ident[:, :])
                    last.then_inc(s_ut, 1)

            def collect(K):
                if K == 1:
                    pe.wait_ge(s_z, 16)
                pe.wait_ge(s_uv, 8 * K + 8)
                pe.wait_ge(s_ua, 8 * K + 8)
                for q in range(16):
                    b = q // 2
                    if q % 2 == 0:
                        pe.wait_ge(s_wl[b % 2], 16 * (4 * K + b // 2 + 1))
                    if q >= 2:
                        pe.wait_ge(s_vr, 16 * K + q - 1)
                        pe.wait_ge(s_vi, 16 * K + q - 1)
                    for g in range(4 * q, 4 * q + 4):
                        last = nc.tensor.matmul(AX2[q % 2][:, P * (g % 4):P * (g % 4) + P],
                                                wb[b % 2][:, P * (g % 8):P * (g % 8) + P],
                                                U[K][:, P * g:P * g + P], start=True, stop=True)
                    last.then_inc(s_v, 1)

            pe.wait_ge(s_pow, 1)
            for j, v in enumerate((16, 17, 18, 19)):
                last = nc.tensor.transpose(AX2[0][:, PR * j:PR * j + PR], pv[:, v, :], ident[0:PR, 0:PR])
            last.then_inc(s_pt, 1)
            transpose_x(0)
            transpose_x(1)
            product_u(0)
            pe.wait_ge(s_c, 16 * 16)
            for r in range(2):
                dst = AX2[1] if r == 0 else UP[1]
                for t in range(4):
                    last = nc.tensor.transpose(dst[:, P * t:P * t + P], Cn[:, r, t, :], ident[:, :])
                last.then_inc(s_ct, 1)
            pe.wait_ge(s_cc, 2)

            for i in range(1, TAU):
                transpose_x(i + 1)
                product_u(i)
            for q in range(16):
                pe.wait_ge(s_Wr, (2 * q + 1) // 8 + 1)
                if q >= 2:
                    pe.wait_ge(s_wc, 2 * (q - 1))
                for l in range(2):
                    for r in range(2):
                        last = nc.tensor.transpose(AX2[q % 2][:, 256 * l + P * r:256 * l + P * r + P],
                                                   Wst[:, r, 2 * q + l].rearrange("p t c -> p (t c)"), ident[:, :])
                last.then_inc(s_wt, 1)
            pe.wait_ge(s_Gr, 2)
            pe.wait_ge(s_wc, 32)
            for q in range(16):
                if q >= 2:
                    pe.wait_ge(s_kc, q - 1)
                rows = slice(N * (q % 2), N * (q % 2) + N)
                for l in range(4):
                    pr = 4 * (q // 2) + l
                    for r in range(2):
                        last = nc.tensor.matmul(AX2[q % 2][0:C, P * l:P * l + P], Bb[rows, r, pr, :],
                                                Gst[rows, r, pr, 0:TAU, :].rearrange("p j c -> p (j c)"),
                                                start=(r == 0), stop=(r == 1))
                last.then_inc(s_kr, 1)
            pe.wait_ge(s_krd, 1)
            transpose_u(0)
            collect(0)
            for i in range(TAU, NT):
                if i + 1 < NT:
                    transpose_x(i + 1)
                product_u(i)
            pe.wait_ge(s_vr, 16)
            pe.wait_ge(s_vi, 16)
            pe.wait_ge(s_td, 16 * 8)
            transpose_u(1)

            def read_out(K):
                pe.wait_ge(s_uv, 16)
                pe.wait_ge(s_ua, 16)
                pe.wait_ge(s_scd, K + 1)
                if K == 1:
                    pe.wait_ge(s_lc, TAU)
                for q in range(16):
                    b = q // 2
                    if q % 2 == 0:
                        pe.wait_ge(s_tg[b % 2], 48 * (4 * K + b // 2 + 1))
                    if q >= 2:
                        pe.wait_ge(s_z, 16 * K + q - 1)
                    t = tgb[b % 2]
                    gg = t[:, 1024:2048].rearrange("p (r q x) -> p r q x", r=2, q=4)
                    a = q % 2
                    rows = slice(N * a, N * a + N)
                    for l in range(4):
                        g = 8 * b + 2 * l + a
                        nc.tensor.matmul(AX2[a][:, P * l:P * l + P], U[K][:, P * g:P * g + P],
                                         t[:, P * (g % 8):P * (g % 8) + P], start=(l == 0), stop=False,
                                         skip_group_check=True)
                    for l in range(4):
                        for r in range(2):
                            last = nc.tensor.matmul(AX2[a][:, P * l:P * l + P], St[rows, r, 4 * b + l, 0:128],
                                                    gg[rows, r, l, :], start=False, stop=(r == 1),
                                                    skip_group_check=True)
                    last.then_inc(s_y, 1)

            def transpose_z(i):
                pe.wait_ge(s_z, 16 * (i // TAU + 1))
                if i % TAU == 0:
                    pe.wait_ge(s_hc, i)
                    pe.wait_ge(s_hT, NT)
                else:
                    pe.wait_ge(s_zc, i)
                    if i >= 2:
                        pe.wait_ge(s_hc, i - 1)
                for k in range(DC):
                    last = nc.tensor.transpose(TP[:, P * k:P * k + P],
                                               R2[:, D * (i % TAU) + P * k:D * (i % TAU) + P * k + P], ident[:, :])
                last.then_inc(s_zt, 1)

            def product_vg(i, nh, ks):
                if i == 0:
                    pe.wait_ge(s_wo, 32)
                    pe.wait_ge(s_ue, NT)
                if i >= 1:
                    pe.wait_ge(s_g1, 2 * (i - 1) + nh + 1)
                for k in ks:
                    w = (R1 if k < 4 else R3)[:, 2048 * (k % 4):2048 * (k % 4) + 2048]
                    for vg in range(2):
                        last = nc.tensor.matmul(UP[nh][:, BK * vg:BK * vg + BK], hT[i % 2][:, P * k:P * k + P],
                                                w[:, D * vg + BK * nh:D * vg + BK * nh + BK],
                                                start=(k == 0), stop=(k == DC - 1))
                if k == DC - 1:
                    last.then_inc(s_vg, 1)

            def transpose_hn(i):
                pe.wait_ge(s_hn, i + 1)
                pe.wait_ge(s_zc, min(i + 2, TAU * (i // TAU) + TAU))
                for k in range(DC):
                    last = nc.tensor.transpose(TP[:, P * k:P * k + P], hn2[:, P * k:P * k + P], ident[:, :])
                last.then_inc(s_ht, 1)

            def router(i):
                pe.wait_ge(s_hc, i + 1)
                if i == 0:
                    pe.wait_ge(s_wrl, 32)
                    pe.wait_ge(s_vr, 32)
                    pe.wait_ge(s_vi, 32)
                if i == TAU:
                    pe.wait_ge(s_z, 32)
                if i >= 1:
                    pe.wait_ge(s_lc, i)
                for k in range(DC):
                    last = nc.tensor.matmul(AX2[0][:, 0:GR + NE], hn2T[:, P * k:P * k + P], wr[:, k, :],
                                            start=(k == 0), stop=(k == DC - 1))
                last.then_inc(s_lg, 1)

            for K in range(2):
                read_out(K)
                if K == 0:
                    pe.wait_ge(s_s0, 2)
                    collect(1)
                t0 = TAU * K
                transpose_z(t0)
                for i in range(t0, t0 + TAU):
                    pe.wait_ge(s_zc, i + 1)
                    product_vg(i, 0, range(DC))
                    if i > t0:
                        transpose_hn(i - 1)
                    product_vg(i, 1, range(4))
                    if i > t0:
                        router(i - 1)
                    if i + 1 < t0 + TAU:
                        transpose_z(i + 1)
                    product_vg(i, 1, range(4, DC))
                transpose_hn(t0 + TAU - 1)
                router(t0 + TAU - 1)

            pe.wait_ge(s_rt, 4)
            pe.wait_ge(s_tri, 6)
            pe.wait_ge(s_lc, NT)
            nc.tensor.matmul(AX2[0][:, :], tri, rt_M.rearrange("p i e -> p (i e)"), start=True, stop=False)
            nc.tensor.matmul(AX2[0][:, :], ones, rt_P.rearrange("p i e -> p (i e)"), start=False, stop=True)
            nc.tensor.matmul(AX2[1][:, 0:NE], ones, rt_tot, start=True, stop=True).then_inc(s_rk, 1)
            for i in range(NT):
                if i % 4 == 0:
                    pe.wait_ge(s_oh, i // 4 + 1)
                for j in range(2):
                    last = nc.tensor.matmul(AX2[1][:, 0:NBT], ohP[:, i, j, :], ohB[:, i, j, :],
                                            start=(i + j == 0), stop=(i == NT - 1 and j == 1))
            last.then_inc(s_tb, 1)
            pe.wait_ge(s_rt, 5)
            for v in range(3):
                last = nc.tensor.matmul(AX2[0][0:1, P * v:P * v + P], rt_eb[:, v:v + 1], ident[:, :], start=True, stop=True)
            last.then_inc(s_tb, 1)


AT = {}
_end = 0
for _name, _n in (("R1", 8192), ("R3", 8192), ("R2", 8192), ("R5", 9216), ("R4", 8192), ("R6", 4096), ("R7", 6144)):
    AT[_name] = (_end, _end + _n)
    _end += _n
ARENA = _end

RAW, RING, NPC, PC = 3, 8, 6, 2048
EARLY = 4
HP = 6


class Region:

    def __init__(self, nc, ctx):
        base = -(-nc.sbuf_base // 32) * 32
        self.arena = ctx.enter_context(nc.sbuf_tensor("arena", [P, ARENA], F32))
        assert nc.sbuf_base == base + 4 * ARENA
        self.nc, self.base = nc, base
        assert AT["R7"][1] - AT["R7"][0] == RAW * PC
        self.raw = [self.own(f"raw{j}", AT["R7"][0] + PC * j, PC, F32) for j in range(RAW)]
        split = self.own("split", 0, 2 * RING * PC, F32R)
        self.wH, self.wL = split, split[:, PC:]
        sem = lambda name: ctx.enter_context(nc.semaphore(name))
        self.s_raw = [sem(f"piece_loaded{j}") for j in range(RAW)]
        self.s_pH = sem("pieces_high")
        self.s_pL = sem("pieces_split")
        self.s_h = [sem(f"h_loaded{j}") for j in range(NT)]

    def __call__(self, name):
        return self.arena[:, AT[name][0]:AT[name][1]]

    def own(self, name, at, n, dt):
        return self.nc.alloc_sbuf_tensor_at(name, [P, n], dt, offset=self.base + 4 * at)[:, :]

    def load_piece(self, sp, weights, e, j):
        w1, w3, w2 = weights
        row = bass.ds(e, 1)
        dst = self.raw[j % RAW].rearrange("p (k n) -> p k n", k=2)
        for half in range(2):
            if j < 4:
                src = (w1, w3)[half].rearrange("e (k p) f -> p e k f", p=P)[:, row, 2 * j:2 * j + 2, :]
                sp.dma_start(dst[:, :, FF * half:FF * half + FF],
                             src.rearrange("p e k f -> p (e k) f")).then_inc(self.s_raw[j % RAW], 16)
            else:
                src = w2.rearrange("e (k p) f -> p e k f", p=P)[:, row, 2 * (j - 4) + half, :]
                sp.dma_start(dst[:, half, :], src.rearrange("p e f -> p (e f)")).then_inc(self.s_raw[j % RAW], 16)


def h_tile(region, i):
    at = AT["R7"][0] + D * i if i < HP else D * (i - HP)
    return region.arena[:, at:at + D]


def build_experts(nc, weights, hn_d, h_d, y_d, ident, rows, blk, region):
    ctx = ExitStack()
    with ctx:
        def sb(name, shape, dt=F32):
            return ctx.enter_context(nc.sbuf_tensor(name, shape, dt))

        def sem(name):
            return ctx.enter_context(nc.semaphore(name))

        raw, wH, wL = region.raw, region.wH, region.wL
        free = [2 * RING * PC]

        def part(name, n, dt=F32):
            at = free[0]
            free[0] += n
            assert free[0] <= AT["R7"][0]
            return region.own(name, at, n, dt)

        xg = [part(f"xg{j}", D) for j in range(2)]
        xH = [part(f"xH{j}", D, F32R) for j in range(2)]
        xL = [part(f"xL{j}", D, F32R) for j in range(2)]
        token = sb("token", [P, NBT], I32)
        idx = [sb(f"idx{j}", [P, 1], I32) for j in range(2)]
        odx = [sb(f"odx{j}", [P, 1], I32) for j in range(2)]
        after = sb("after", [1, 1])
        sil = part("sil", FF)
        hm = part("hm", FF)
        hH = part("hH", FF, F32R)
        hL = part("hL", FF, F32R)
        yo = [part(f"yo{j}", D) for j in range(2)]
        XB = ctx.enter_context(nc.psum_tensor("XB", [P, BK], F32))
        HB = ctx.enter_context(nc.psum_tensor("HB", [P, BK], F32))
        H13 = [ctx.enter_context(nc.psum_tensor(f"H13_{j}", [P, 2 * BK], F32)) for j in range(2)]
        YB = ctx.enter_context(nc.psum_tensor("YB", [P, 2 * BK], F32))

        s_raw, s_pH, s_pL = region.s_raw, region.s_pH, region.s_pL
        s_xg = [sem(f"rows_gathered{j}") for j in range(2)]
        s_tok = sem("tokens_ready")
        s_idx = sem("indices_ready")
        s_odx = sem("y_indices_ready")
        s_xt = sem("rows_transposed")
        s_xH = sem("rowsT_high")
        s_xL = sem("rowsT_split")
        s_1 = sem("first_product")
        s_sil = sem("silu_ready")
        s_hm = sem("hidden_ready")
        s_ht = sem("hidden_transposed")
        s_hH = sem("hiddenT_high")
        s_hL = sem("hiddenT_split")
        s_2 = sem("second_product")
        s_yA = sem("y_copied_act")
        s_yV = sem("y_copied_dve")
        s_ys = [sem(f"y_stored{j}") for j in range(2)]

        block = ctx.enter_context(nc.Block())
        word = lambda eng, j, hi: eng.value_load(blk[0:1, bass.ds(j, 1)], min_val=0, max_val=hi)
        last_block = lambda eng: eng.value_load(blk[0:1, 3 * NBT:3 * NBT + 1], min_val=0, max_val=NB - 1)

        @block.sync
        def _(sp):
            with sp.Fori(0, NE - 1) as i:
                for j in range(NPC):
                    sp.wait_ge(s_pL, NPC * i + (NPC + j + 1 - RAW))
                    region.load_piece(sp, weights, i + 1, j)
            assert D * (NT - HP) <= 3 * 2 * PC and (NPC * NE) % RING == 0
            last = last_block(sp)
            sp.wait_ge(s_pL, NPC * NE)
            for i in range(NT):
                if i == HP:
                    sp.wait_ge(s_1, last + 1)
                sp.dma_start(h_tile(region, i), tile_rows(h_d, i // TAU, i % TAU)).then_inc(region.s_h[i], 16)

        @block.gpsimd
        def _(pool):
            def gather(x, j, later):
                if later:
                    pool.wait_ge(s_xt, 2 * x - 2)
                nc.gpsimd.tensor_copy(idx[j][:, :], token[:, bass.ds(x, 1)]).then_inc(s_idx, 1)
                pool.wait_ge(s_idx, x + 1)
                nc.gpsimd.tensor_tensor(out=after[:, :], in0=ident[0:1, 0:1], in1=ident[0:1, 0:1], op=ALU.add)
                pool.indirect_dma_start(out=xg[j][:, :], out_offset=None, in_=hn_d,
                                        in_offset=bass.IndirectOffsetOnAxis(ap=idx[j][:, :], axis=0)
                                        ).then_inc(s_xg[j], 16)

            def scatter(y, j):
                pool.wait_ge(s_yA, y + 1)
                pool.wait_ge(s_yV, y + 1)
                nc.gpsimd.tensor_copy(odx[j][:, :], rows[:, bass.ds(y, 1)]).then_inc(s_odx, 1)
                pool.wait_ge(s_odx, y + 1)
                nc.gpsimd.tensor_tensor(out=after[:, :], in0=ident[0:1, 0:1], in1=ident[0:1, 0:1], op=ALU.add)
                pool.indirect_dma_start(out=y_d, out_offset=bass.IndirectOffsetOnAxis(ap=odx[j][:, :], axis=0),
                                        in_=yo[j][:, :], in_offset=None).then_inc(s_ys[j], 16)

            pool.wait_ge(s_tok, 1)
            gather(0, 0, False)
            gather(1, 1, False)
            last = last_block(pool)
            with pool.Fori(0, NB // 2) as i:
                for j in range(2):
                    with pool.If(2 * i + j < last + 1):
                        gather(2 * i + j + 2, j, True)
                        scatter(2 * i + j, j)
                        pool.nop()
            pool.wait_ge(s_ys[0], 16 * ((last + 2) // 2))
            pool.wait_ge(s_ys[1], 16 * ((last + 1) // 2))
            for j in range(2):
                pool.wait_ge(s_xg[j], 16)

        @block.scalar
        def _(act):
            def high(e, j):
                act.wait_ge(s_raw[j % RAW], 32 * (2 * e + j // RAW + 1))
                slot = 2 * ((NPC * e + j) % RING)
                out = wH[:, bass.ds(slot * PC, PC)] if not isinstance(slot, int) else wH[:, slot * PC:slot * PC + PC]
                nc.scalar.activation(out, raw[j % RAW][:, :], ACT.Copy).then_inc(s_pH, 1)

            def rows_high(x, j, half, later):
                act.wait_ge(s_xt, 2 * x + half + 1)
                if later:
                    act.wait_ge(s_1, x - 1)
                nc.scalar.activation(xH[j][:, BK * half:BK * half + BK], XB[:, :], ACT.Copy).then_inc(s_xH, 1)

            def hidden_high(y):
                act.wait_ge(s_ht, y + 1)
                act.wait_ge(s_2, y)
                nc.scalar.activation(hH[:, :], HB[:, :], ACT.Copy).then_inc(s_hH, 1)

            def silu(g, j):
                act.wait_ge(s_1, g + 1)
                act.wait_ge(s_hm, g)
                nc.scalar.activation(sil[:, :], H13[j][:, 0:BK], ACT.Silu).then_inc(s_sil, 1)

            def copy_y(y, j):
                act.wait_ge(s_2, y + 1)
                act.wait_ge(s_ys[j], 16 * (y // 2))
                nc.scalar.activation(yo[j][:, 0:BK], YB[:, 0:BK], ACT.Copy).then_inc(s_yA, 1)

            for j in range(EARLY, NPC):
                high(0, j)
            for half in range(2):
                rows_high(0, 0, half, False)
            for j in range(2):
                high(1, j)

            def step(g, j, peeled):
                e = word(act, g, NE - 1)
                last = word(act, NBT + g, 1)
                if not peeled:
                    new = word(act, NBT + g - 1, 1)
                    freed = word(act, 2 * NBT + g - 1, 1)
                    hidden_high(g - 1)
                    with act.If(new > 0):
                        high(e, 3)
                        act.nop()
                rows_high(g + 1, 1 - j, 0, not peeled)
                if not peeled:
                    with act.If(new > 0):
                        high(e, 4)
                        high(e, 5)
                        act.nop()
                    copy_y(g - 1, 1 - j)
                rows_high(g + 1, 1 - j, 1, not peeled)
                if not peeled:
                    before = word(act, g - 1, NE - 1)
                    with act.If(freed > 0):
                        high(before + 2, 0)
                        high(before + 2, 1)
                        act.nop()
                silu(g, j)
                with act.If(last > 0):
                    high(e + 1, 2)
                    act.nop()

            step(0, 0, True)
            last = last_block(act)
            with act.Fori(0, NB // 2) as i:
                for j in range(2):
                    x = 2 * i + j
                    with act.If(x < last + 1):
                        with act.If(x < last):
                            step(x + 1, 1 - j, False)
                            act.nop()
                        with act.Else():
                            hidden_high(x)
                            copy_y(x, j)
                            act.nop()
                        act.nop()

        @block.vector
        def _(dve):
            sub = lambda out, a, h: nc.vector.tensor_tensor(out=out, in0=a, in1=h.bitcast(F32), op=ALU.subtract)

            def low(e, j):
                dve.wait_ge(s_pH, NPC * e + j + 1)
                slot = 2 * ((NPC * e + j) % RING)
                at = bass.ds(slot * PC, PC) if not isinstance(slot, int) else slice(slot * PC, slot * PC + PC)
                sub(wL[:, at], raw[j % RAW][:, :], wH[:, at]).then_inc(s_pL, 1)

            def rows_low(x, j, half):
                dve.wait_ge(s_xH, 2 * x + half + 1)
                f = slice(BK * half, BK * half + BK)
                sub(xL[j][:, f], XB[:, :], xH[j][:, f]).then_inc(s_xL, 1)

            def hidden_low(y):
                dve.wait_ge(s_hH, y + 1)
                sub(hL[:, :], HB[:, :], hH[:, :]).then_inc(s_hL, 1)

            def hidden(g, j):
                dve.wait_ge(s_sil, g + 1)
                dve.wait_ge(s_ht, g)
                nc.vector.tensor_tensor(out=hm[:, :], in0=sil[:, :], in1=H13[j][:, BK:2 * BK], op=ALU.mult).then_inc(s_hm, 1)

            def copy_y(y, j):
                dve.wait_ge(s_2, y + 1)
                dve.wait_ge(s_ys[j], 16 * (y // 2))
                nc.vector.tensor_copy(yo[j][:, BK:D], YB[:, BK:2 * BK]).then_inc(s_yV, 1)

            nc.vector.tensor_scalar(token[:, :], rows[:, :], S - 1, None, ALU.bitwise_and).then_inc(s_tok, 1)
            for j in range(EARLY, NPC):
                low(0, j)
            for half in range(2):
                rows_low(0, 0, half)
            for j in range(2):
                low(1, j)

            def step(g, j, peeled):
                e = word(dve, g, NE - 1)
                last = word(dve, NBT + g, 1)
                if not peeled:
                    new = word(dve, NBT + g - 1, 1)
                    freed = word(dve, 2 * NBT + g - 1, 1)
                    hidden_low(g - 1)
                    with dve.If(new > 0):
                        low(e, 3)
                        dve.nop()
                rows_low(g + 1, 1 - j, 0)
                if not peeled:
                    with dve.If(new > 0):
                        low(e, 4)
                        low(e, 5)
                        dve.nop()
                    copy_y(g - 1, 1 - j)
                rows_low(g + 1, 1 - j, 1)
                if not peeled:
                    before = word(dve, g - 1, NE - 1)
                    with dve.If(freed > 0):
                        low(before + 2, 0)
                        low(before + 2, 1)
                        dve.nop()
                hidden(g, j)
                with dve.If(last > 0):
                    low(e + 1, 2)
                    dve.nop()

            step(0, 0, True)
            last = last_block(dve)
            with dve.Fori(0, NB // 2) as i:
                for j in range(2):
                    x = 2 * i + j
                    with dve.If(x < last + 1):
                        with dve.If(x < last):
                            step(x + 1, 1 - j, False)
                            dve.nop()
                        with dve.Else():
                            hidden_low(x)
                            copy_y(x, j)
                            dve.nop()
                        dve.nop()

        @block.tensor
        def _(pe):
            def transpose_rows(x, j, half):
                if half == 0:
                    pe.wait_ge(s_xg[j], 16 * (x // 2 + 1))
                if not isinstance(x, int) or 2 * x + half > 0:
                    pe.wait_ge(s_xL, 2 * x + half)
                for k in range(4):
                    f = BK * half + P * k
                    last = nc.tensor.transpose(XB[:, P * k:P * k + P], xg[j][:, f:f + P], ident[:, :])
                last.then_inc(s_xt, 1)

            def three(out, aH, aL, at, start, stop):
                nc.tensor.matmul(out, aH, wH[:, at], start=start, stop=False)
                nc.tensor.matmul(out, aH, wL[:, at], start=False, stop=False)
                return nc.tensor.matmul(out, aL, wH[:, at], start=False, stop=stop)

            def piece(e, jp):
                slot = 2 * ((NPC * e + jp) % RING)
                return slot * PC if isinstance(slot, int) else pe.snap(slot * PC)

            def tile(base, k, n):
                o = base + n * BK + (k % 2) * 2 * BK
                return slice(o, o + BK) if isinstance(o, int) else bass.ds(o, BK)

            def first(e, j, jp):
                pe.wait_ge(s_pL, NPC * e + jp + 1)
                base = piece(e, jp)
                for k in (2 * jp, 2 * jp + 1):
                    kk = slice(P * k, P * k + P)
                    for n in range(2):
                        last = three(H13[j][:, BK * n:BK * n + BK], xH[j][:, kk], xL[j][:, kk], tile(base, k, n),
                                     k == 0, k == DC - 1)
                return last

            def transpose_hidden(y):
                pe.wait_ge(s_hm, y + 1)
                pe.wait_ge(s_hL, y)
                for k in range(FC):
                    last = nc.tensor.transpose(HB[:, P * k:P * k + P], hm[:, P * k:P * k + P], ident[:, :])
                last.then_inc(s_ht, 1)

            def second(e, y):
                pe.wait_ge(s_hL, y + 1)
                pe.wait_ge(s_yA, y)
                pe.wait_ge(s_yV, y)
                for jp in (4, 5):
                    pe.wait_ge(s_pL, NPC * e + jp + 1)
                    base = piece(e, jp)
                    for k in (2 * jp - 8, 2 * jp - 7):
                        kk = slice(P * k, P * k + P)
                        for n in range(2):
                            last = three(YB[:, BK * n:BK * n + BK], hH[:, kk], hL[:, kk], tile(base, k, n),
                                         k == 0, k == FC - 1)
                last.then_inc(s_2, 1)

            def step(g, j, peeled):
                e = word(pe, g, NE - 1)
                if not peeled:
                    before = word(pe, g - 1, NE - 1)
                pe.wait_ge(s_xL, 2 * g + 2)
                if not isinstance(g, int):
                    pe.wait_ge(s_hm, g - 1)
                first(e, j, 0)
                if not peeled:
                    transpose_hidden(g - 1)
                first(e, j, 1)
                transpose_rows(g + 1, 1 - j, 0)
                if not peeled:
                    second(before, g - 1)
                transpose_rows(g + 1, 1 - j, 1)
                first(e, j, 2)
                first(e, j, 3).then_inc(s_1, 1)

            transpose_rows(0, 0, 0)
            transpose_rows(0, 0, 1)
            step(0, 0, True)
            last = last_block(pe)
            with pe.Fori(0, NB // 2) as i:
                for j in range(2):
                    x = 2 * i + j
                    with pe.If(x < last + 1):
                        with pe.If(x < last):
                            step(x + 1, 1 - j, False)
                            pe.nop()
                        with pe.Else():
                            transpose_hidden(x)
                            second(NE - 1, x)
                            pe.nop()
                        pe.nop()


def build_combine(nc, ln_final, h_d, y_d, out, gates, region):
    Y = 12
    ctx = ExitStack()
    with ctx:
        def sb(name, shape, dt=F32):
            return ctx.enter_context(nc.sbuf_tensor(name, shape, dt))

        def sem(name):
            return ctx.enter_context(nc.semaphore(name))

        ht = [h_tile(region, i) for i in range(NT)]
        at = D * (NT - HP)
        tiles = [region.arena[:, at + D * j:at + D * j + D] for j in range(2 * Y + 2)]
        assert at + D * len(tiles) <= AT["R7"][0]
        ya = [tiles[2 * j:2 * j + 2] for j in range(Y)]
        sq, gB = tiles[2 * Y:]
        st = sb("st", [P, 2 * NT])
        mh = sb("mh", [P, 1])
        s_h = region.s_h
        s_ya = [sem(f"rows_loaded{j}") for j in range(Y)]
        s_g = sem("final_gain_loaded")
        s_mh = sem("minus_half")
        s_sum = sem("sums")
        s_sq = sem("final_squares")
        s_rs = sem("final_rstd")
        s_o = sem("out_ready")
        s_od = sem("out_stored")
        block = ctx.enter_context(nc.Block())

        @block.sync
        def _(sp):
            def load(i):
                if i >= Y:
                    sp.wait_ge(s_sum, 2 * (i - Y) + 2)
                for r in range(2):
                    src = y_d[S * r:S * r + S]
                    sp.dma_start(ya[i % Y][r][:, :], tile_rows(src, i // TAU, i % TAU)).then_inc(s_ya[i % Y], 16)

            for i in range(NT):
                load(i)
            sp.wait_ge(s_od, 16 * NT)

        @block.gpsimd
        def _(pool):
            nc.gpsimd.memset(mh[:, :], -0.5).then_inc(s_mh, 1)
            pool.wait_ge(s_mh, 1)

            for i in range(NT):
                pool.wait_ge(s_sq, i + 1)
                nc.gpsimd.tensor_scalar(st[:, NT + i:NT + i + 1], st[:, i:i + 1], 1.0 / D, EPS, ALU.mult, ALU.add).then_inc(s_rs, 1)
                pool.wait_ge(s_rs, 2 * i + 1)
                nc.gpsimd.tensor_tensor(out=st[:, NT + i:NT + i + 1], in0=st[:, NT + i:NT + i + 1], in1=mh[:, 0:1], op=ALU.pow).then_inc(s_rs, 1)

        @block.scalar
        def _(act):
            act.dma_start(gB[:, :], ln_final.partition_broadcast(P)).then_inc(s_g, 16)

            def store(i):
                act.wait_ge(s_o, i + 1)
                act.dma_start(tile_rows(out, i // TAU, i % TAU), ht[i]).then_inc(s_od, 16)

            for i in range(NT):
                act.wait_ge(s_sum, 2 * i + 2)
                if i > 0:
                    act.wait_ge(s_sq, i)
                nc.scalar.activation(sq[:, :], ht[i][:, :], ACT.Square, accum_out=st[:, i:i + 1]).then_inc(s_sq, 1)
                if i >= 1:
                    store(i - 1)
            store(NT - 1)

        @block.vector
        def _(dve):
            dve.wait_ge(s_g, 16)

            def add(i):
                h = ht[i][:, :]
                dve.wait_ge(s_h[i], 16)
                dve.wait_ge(s_ya[i % Y], 32 * (i // Y + 1))
                for r in range(2):
                    nc.vector.scalar_tensor_tensor(out=h, in0=ya[i % Y][r][:, :], scalar=gates[:, i, r:r + 1], in1=h,
                                                   op0=ALU.mult, op1=ALU.add).then_inc(s_sum, 1)
                    dve.wait_ge(s_sum, 2 * i + r + 1)

            add(0)
            for i in range(NT):
                if i + 1 < NT:
                    add(i + 1)
                dve.wait_ge(s_rs, 2 * i + 2)
                nc.vector.scalar_tensor_tensor(out=ht[i][:, :], in0=ht[i][:, :], scalar=st[:, NT + i:NT + i + 1],
                                               in1=gB[:, :], op0=ALU.mult, op1=ALU.mult).then_inc(s_o, 1)


def build(nc, a, out):
    W_d = nc.dram_tensor("W_d", [8 * P, 1024], F32).ap()
    T_d = nc.dram_tensor("T_d", [P, 8 * 1024], F32).ap()
    G_d = nc.dram_tensor("G_d", [2 * P, 8 * 512], F32).ap()
    h_d = nc.dram_tensor("h_d", [S, D], F32).ap()
    hn_d = nc.dram_tensor("hn_d", [S, D], F32).ap()
    y_d = nc.dram_tensor("y_d", [2 * S + P * NBT, D], F32).ap()
    with ExitStack() as ctx:
        sb = lambda name, shape, dt: ctx.enter_context(nc.sbuf_tensor(name, shape, dt))
        ident = sb("ident", [P, P], F32)
        rows = sb("rows", [P, NBT], I32)
        gates = sb("gates", [P, NT, 2], F32)
        blk = sb("blk", [1, 3 * NBT + 1], I32)
        one = lambda k: a[k][0]
        region = Region(nc, ctx)
        weights = (one("moe_w1"), one("moe_w3"), one("moe_w2"))
        build_mixer(nc, a["x"][0], one("ln_mix"), one("ln_ffn"), one("ssm_w_in"), one("ssm_lam_re"), one("ssm_lam_im"),
                    one("ssm_log_dt"), one("ssm_b_re"), one("ssm_b_im"), one("ssm_c_re"), one("ssm_c_im"), one("ssm_d"),
                    one("ssm_w_out"), one("moe_w_group"), one("moe_w_expert"), h_d, hn_d, W_d, T_d, G_d,
                    ident, rows[:, :], gates[:, :, :], blk[:, :], region, weights)
        build_experts(nc, weights, hn_d, h_d, y_d, ident, rows, blk, region)
        build_combine(nc, a["ln_final"], h_d, y_d, out[0], gates, region)


_INS = ["x", "ln_mix", "ln_ffn", "ln_final", "ssm_w_in", "ssm_lam_re", "ssm_lam_im", "ssm_log_dt", "ssm_b_re", "ssm_b_im",
        "ssm_c_re", "ssm_c_im", "ssm_d", "ssm_w_out", "moe_w_group", "moe_w_expert", "moe_w1", "moe_w3", "moe_w2"]


def kernel(**inputs):
    import numpy as _np
    import concourse.bacc as _bacc
    from concourse import mybir as _mybir
    from concourse.bass_utils import run_bass_kernel_spmd as _run

    nc = _bacc.Bacc("TRN2", target_bir_lowering=False, num_devices=1)
    arrays, aps = {}, {}
    for name in _INS:
        v = _np.ascontiguousarray(inputs[name])
        arrays[f"in_{name}"] = v
        aps[name] = nc.dram_tensor(f"in_{name}", v.shape, _mybir.dt.from_np(v.dtype), kind="ExternalInput").ap()
    out = nc.dram_tensor("out_0", (1, S, D), F32, kind="ExternalOutput").ap()
    build(nc, aps, out)
    r = _run(nc, [arrays], core_ids=[0])
    return r.results[0]["out_0"]
```
